# Optimizing a Trainium2 kernel written in Bass

```python
import math
import jax, jax.numpy as jnp
from jax import lax
import numpy as np

D_MODEL = 2048
BATCH = 1
SEQ = 256
DEPTH = 1

EPS = 1e-6
CHUNK = 128
A_GROUPS = 8
A_WIDTH = 1024
A_GROUP_DIM = A_WIDTH // A_GROUPS
B_WIDTH = 1024
SHORT_CONV = 3
ATTN_HEADS = 8
ATTN_HEAD_DIM = 128
C_WIDTH = ATTN_HEADS * ATTN_HEAD_DIM
IDX_HEADS = 16
IDX_HEAD_DIM = 64
TOPK_MAX = 256
Q_BLOCK = 128
NUM_BUCKETS = 32
MAX_DISTANCE = 128
NEG_INF = -1e30

SECTION_SIZES = (
    A_WIDTH, A_WIDTH, A_WIDTH,
    B_WIDTH, B_WIDTH, B_WIDTH, B_WIDTH,
    C_WIDTH, C_WIDTH, C_WIDTH, C_WIDTH,
    IDX_HEADS * IDX_HEAD_DIM, IDX_HEAD_DIM, IDX_HEADS,
    D_MODEL, D_MODEL, D_MODEL,
)
IN_COLS = 18512

kernel_name = "hybrid_gated_sgu_shortconv_dsa"

def rmsnorm(x, g):
    xf = x.astype(jnp.float32)
    y = xf * lax.rsqrt(jnp.mean(xf * xf, axis=-1, keepdims=True) + EPS)
    return (y * g.astype(jnp.float32)).astype(x.dtype)

def t5_bucket(dist):
    n = jnp.maximum(dist, 0)
    max_exact = NUM_BUCKETS // 2
    nf = jnp.maximum(n, 1).astype(jnp.float32)
    large = max_exact + (jnp.log(nf / max_exact) / math.log(MAX_DISTANCE / max_exact)
                         * (NUM_BUCKETS - max_exact)).astype(jnp.int32)
    large = jnp.minimum(large, NUM_BUCKETS - 1)
    return jnp.where(n < max_exact, n, large)

def split_columns(p):
    outs = []
    off = 0
    for size in SECTION_SIZES:
        outs.append(p[..., off:off + size])
        off += size
    return outs

def spatial_gating(u, v, ws, bias):
    b_, L, _ = v.shape
    n_chunks = L // CHUNK
    mask = jnp.tril(jnp.ones((CHUNK, CHUNK), dtype=bool))
    ws = jnp.where(mask[None], ws, jnp.zeros_like(ws))
    v5 = v.reshape(b_, n_chunks, CHUNK, A_GROUPS, A_GROUP_DIM)
    mixed = jnp.einsum('gts,bnsgc->bntgc', ws, v5) + bias.T[None, None, :, :, None]
    return u * mixed.reshape(b_, L, A_WIDTH)

def short_gated_conv(gate_b, gate_c, x_in, conv_w):
    cx = gate_c * x_in
    conv = lax.conv_general_dilated(
        cx, conv_w[:, None, :].astype(cx.dtype), window_strides=(1,),
        padding=[(SHORT_CONV - 1, 0)], dimension_numbers=('NWC', 'WIO', 'NWC'),
        feature_group_count=B_WIDTH)
    return gate_b * conv

def dsa_attention(q, k, v, iq, ik, iw, rel_bias, topk):
    b_, L, _ = q.shape
    nb = L // Q_BLOCK
    qb_all = q.reshape(b_, nb, Q_BLOCK, ATTN_HEADS, ATTN_HEAD_DIM).swapaxes(0, 1)
    iq_all = iq.reshape(b_, nb, Q_BLOCK, IDX_HEADS, IDX_HEAD_DIM).swapaxes(0, 1)
    iw_all = (iw * (IDX_HEADS ** -0.5 * IDX_HEAD_DIM ** -0.5)).reshape(
        b_, nb, Q_BLOCK, IDX_HEADS).swapaxes(0, 1)
    k4 = k.reshape(b_, L, ATTN_HEADS, ATTN_HEAD_DIM)
    v4 = v.reshape(b_, L, ATTN_HEADS, ATTN_HEAD_DIM)
    key_pos = jnp.arange(L, dtype=jnp.int32)
    starts = jnp.arange(nb, dtype=jnp.int32) * Q_BLOCK
    scale = ATTN_HEAD_DIM ** -0.5
    gather = jax.vmap(lambda tb, ib: tb[ib])

    def block(args):
        qb, iqb, iwb, start = args
        qpos = start + jnp.arange(Q_BLOCK, dtype=jnp.int32)
        rel = jax.nn.relu(jnp.einsum('bqhd,bsd->bqsh', iqb, ik))
        score = jnp.einsum('bqsh,bqh->bqs', rel, iwb).astype(jnp.float32)
        causal = key_pos[None, None, :] <= qpos[None, :, None]
        score = jnp.where(causal, score, NEG_INF)
        _, idx = lax.top_k(score, topk)
        k_sel = gather(k4, idx)
        v_sel = gather(v4, idx)
        dist = qpos[None, :, None] - idx
        bias = rel_bias[t5_bucket(dist)].astype(jnp.float32)
        logits = jnp.einsum('bqhd,bqkhd->bqhk', qb, k_sel).astype(jnp.float32) * scale
        logits = logits + jnp.transpose(bias, (0, 1, 3, 2))
        logits = jnp.where((dist >= 0)[:, :, None, :], logits, NEG_INF)
        p = jax.nn.softmax(logits, axis=-1)
        return jnp.einsum('bqhk,bqkhd->bqhd', p.astype(v_sel.dtype), v_sel)

    out = lax.map(block, (qb_all, iq_all, iw_all, starts))
    return out.swapaxes(0, 1).reshape(b_, L, C_WIDTH)

def setup_inputs(seed: int = 0) -> dict:
    key = jax.random.key(seed)
    ks = jax.random.split(key, 14)
    f32 = jnp.float32
    nrm = lambda k, shape, s: jax.random.normal(k, shape, f32) * s
    return {
        "x": nrm(ks[0], (BATCH, SEQ, D_MODEL), 1.0),
        "norm_g": 1.0 + nrm(ks[1], (DEPTH, D_MODEL), 0.02),
        "w_in": nrm(ks[2], (DEPTH, D_MODEL, IN_COLS), D_MODEL ** -0.5),
        "a_ws": nrm(ks[3], (DEPTH, A_GROUPS, CHUNK, CHUNK), CHUNK ** -0.5),
        "a_b": 1.0 + nrm(ks[4], (DEPTH, A_GROUPS, CHUNK), 0.1),
        "b_conv": nrm(ks[5], (DEPTH, SHORT_CONV, B_WIDTH), SHORT_CONV ** -0.5),
        "p_a": nrm(ks[6], (DEPTH, A_WIDTH, D_MODEL), A_WIDTH ** -0.5),
        "p_b": nrm(ks[7], (DEPTH, B_WIDTH, D_MODEL), B_WIDTH ** -0.5),
        "p_c": nrm(ks[8], (DEPTH, C_WIDTH, D_MODEL), C_WIDTH ** -0.5),
        "w_o": nrm(ks[9], (DEPTH, D_MODEL, D_MODEL), D_MODEL ** -0.5),
        "rel_bias": nrm(ks[10], (NUM_BUCKETS, ATTN_HEADS), 0.5),
        "final_g": 1.0 + nrm(ks[11], (D_MODEL,), 0.02),
    }

def reference(x, norm_g, w_in, a_ws, a_b, b_conv, p_a, p_b, p_c, w_o, rel_bias, final_g):
    L = x.shape[1]
    topk = min(TOPK_MAX, L // 4)
    for l in range(DEPTH):
        h = rmsnorm(x, norm_g[l])
        proj = jnp.einsum('bsd,de->bse', h, w_in[l])
        (a_u, a_v, a_z, b_bg, b_cg, b_x, b_z, c_q, c_k, c_v, c_z,
         i_q, i_k, i_w, g_a, g_b, g_c) = split_columns(proj)
        y_a = spatial_gating(a_u, a_v, a_ws[l], a_b[l]) * jax.nn.silu(a_z)
        y_b = short_gated_conv(b_bg, b_cg, b_x, b_conv[l]) * jax.nn.silu(b_z)
        y_c = dsa_attention(c_q, c_k, c_v, i_q, i_k, i_w, rel_bias, topk) * jax.nn.silu(c_z)
        m = (jax.nn.sigmoid(g_a) * (y_a @ p_a[l])
             + jax.nn.sigmoid(g_b) * (y_b @ p_b[l])
             + jax.nn.sigmoid(g_c) * (y_c @ p_c[l]))
        x = x + m @ w_o[l]
    return rmsnorm(x, final_g)


_drawn_inputs = setup_inputs


def setup_inputs(seed=0):
    import zlib

    import numpy as np

    out = dict(_drawn_inputs(seed))
    spreads = {}
    factors = {'norm_g': 3.01, 'final_g': 8.444, 'a_b': 5.079, 'rel_bias': 4.338}
    for name, (base, spread) in spreads.items():
        noise = np.random.default_rng([zlib.crc32(name.encode()), seed]).standard_normal(out[name].shape)
        drawn = base * np.exp(spread * noise) if base else spread * noise
        out[name] = __import__('jax').numpy.asarray(drawn.astype(out[name].dtype))
    for name, factor in factors.items():
        out[name] = (out[name] * factor).astype(out[name].dtype)
    return out
```

```python
from contextlib import ExitStack

import concourse.bass as bass
from concourse import mybir

F32 = mybir.dt.float32
F32R = mybir.dt.float32r
ACT = mybir.ActivationFunctionType
ALU = mybir.AluOpType
AX_X = mybir.AxisListType.X

P = 128
SEQ = 256
D = 2048
T = SEQ // P
KD = D // P
WIDTH = 1024
KW = WIDTH // P
HEADS = 8
IDX_HEADS = 16
IDX_DIM = 64
TOPK = 64
BUCKETS = 32
MAX_DISTANCE = 128
TAPS = 3
EPS = 1e-6
NEG = -1e30
TAKEN = -3e38
SCALE = float(P) ** -0.5

N = 512
RING = 4
KS = 2
SUB = KD // KS
SUBP = KW // KS

A_U, A_V, A_Z = 0, 1024, 2048
B_G, B_C, B_X, B_Z = 3072, 4096, 5120, 6144
C_Q, C_K, C_V, C_Z = 7168, 8192, 9216, 10240
I_Q, I_K = 11264, 12288
G_A, G_B, G_C = 12368, 14416, 16464
IKW = IDX_DIM + IDX_HEADS

PHASE1 = [(C_Z, 2), (I_Q, 2)]
PHASE2 = [(C_Q, 6), (B_G, 2)]
PHASE3 = [(B_C, 2)]
PHASE4 = [(B_X, 4)]
PHASE5 = [(A_Z, 2), (A_U, 4), (G_B + 2 * N, 2)]
PHASE6 = [(G_C, 4), (G_A, 4)]
PHASE7 = [(G_B, 2)]

SUB1 = 2
SUB2 = SUB1 + 4 * SUB
SUB3 = SUB2 + 8 * SUB
SUB4 = SUB3 + 2 * SUB
SUB5 = SUB4 + 4 * SUB
SUB6 = SUB5 + 8 * SUB
SUB7 = SUB6 + 8 * SUB
SUBP0 = SUB7 + 2 * SUB
SUBO = SUBP0 + 4 * 3 * SUBP
SUBS = SUBO + 4 * SUB
CH1, CH2, CH3, CH4, CH5, CH6, CH7, CHP, CHO = 1, 5, 13, 15, 19, 27, 35, 37, 49

Q, K, V, BG, BX, BZ = 0, 2, 4, 6, 8, 10
EARLY = 12
CZ, IQ, BC, AZ, YB, AU, AV, GB, GC, GA = 0, 2, 2, 2, 2, 4, 6, 6, 10, 14
KEEP = 18


def trunk(nc, x, norm_g, w_in, a_ws, a_b, b_conv, p_a, p_b, p_c, w_o, rel_bias, final_g,
          identity, flip, buckets, out):
    table_dram = nc.dram_tensor("bias_table", (HEADS, N), F32).ap()
    rows = lambda w: w.rearrange("(k p) n -> p k n", p=P)
    w_in_v, w_o_v = rows(w_in[0]), rows(w_o[0])
    p_v = [rows(p_c[0]), rows(p_a[0]), rows(p_b[0])]
    x_v = x[0].rearrange("(t p) d -> p t d", p=P)
    out_v = out[0].rearrange("(t p) d -> p t d", p=P)

    with ExitStack() as ctx:
        def sb(name, shape, dt=F32):
            return ctx.enter_context(nc.sbuf_tensor(name, shape, dt))

        def sem(name):
            return ctx.enter_context(nc.semaphore(name))

        raw = sb("raw", [P, RING, KS * N])
        wh = sb("wh", [P, RING, KS * N], F32R)
        wl = sb("wl", [P, RING, KS * N], F32R)
        hh = sb("hh", [P, KD, SEQ], F32R)
        hl = sb("hl", [P, KD, SEQ], F32R)
        guard = nc.sbuf_tensor("early", [P, T, EARLY * N], F32)
        early = guard.__enter__()
        guard.__exit__(None, None, None)
        yh = sb("yh", [P, 3 * KW, SEQ], F32R)
        yl = sb("yl", [P, 3 * KW, SEQ], F32R)
        keep = sb("keep", [P, T, KEEP * N])
        ws_t = sb("ws_t", [P, KW, P])
        ident = sb("ident", [P, P])
        ik_t = sb("ik_t", [P, SEQ])
        iw = sb("iw", [P, T, IDX_HEADS])
        ab_t = sb("ab_t", [P, KW])
        conv_t = sb("conv_t", [P, TAPS, KW])
        stats = sb("stats", [P, 48])
        psum = ctx.enter_context(nc.psum_tensor("psum", [P, 8, N], F32))
        acc = [psum[:, t] for t in range(T)]
        bank = [psum[:, 2 + i] for i in range(6)]
        acc_p = [[psum[:, T * b + t] for t in range(T)] for b in range(3)]
        bank_m = [psum[:, 6 + i] for i in range(2)]

        def section(buf, slot, n=2):
            return buf[:, :, slot * N:(slot + n) * N]

        def chunk(buf, slot, t):
            return buf[:, t, bass.ds(slot * N, N)]

        def block(buf, slot, i):
            return buf[:, :, bass.ds(slot * N + i * P, P)]

        def blk(ap):
            return ap.rearrange("p (a c) -> p a c", c=P)

        x_s = section(keep, 4, 4)
        g_all = keep[:, 0, 8 * N:12 * N]
        xn = section(keep, 12, 4)
        ws_s = early[:, 0, 0:KW * P]
        small = early[:, 0, 2048:2048 + P]
        onehot = early[0:BUCKETS, 0, 2560:2560 + N]
        rel = early[0:BUCKETS, 0, 3072:3072 + HEADS]
        table = early[0:HEADS, 0, 3584:3584 + N]
        flip_s = early[:, 0, 4096:4096 + P]
        ik_s = early[:, 0, 4608:4608 + T * P]
        bias_rev = keep[:, 1, 8 * N:12 * N]
        bias = keep[:, 0, 8 * N:12 * N].rearrange("p (h s) -> p h s", h=HEADS)
        bias_m = keep[:, 0, 12 * N:18 * N].rearrange("p (h s) -> p h s", h=HEADS)
        score = keep[:, 0, 4 * N:4 * N + 384]
        relu = keep[:, 0, 5 * N:5 * N + 768].rearrange("p (h s) -> p h s", h=2)
        iq_s = keep[:, 1, 4 * N:4 * N + SEQ].rearrange("p (t c) -> p t c", t=T)
        iq_t = keep[:, 1, 5 * N:5 * N + SEQ]
        mask = keep[:, 1, 6 * N:6 * N + 384]
        top8 = stats[:, 0:16].rearrange("p (b c) -> p b c", b=2)
        qk_s = keep[:, 1, 12 * N:13 * N].rearrange("p (w t c) -> p w t c", w=2, t=T)
        qk_t = keep[:, 1, 13 * N:14 * N]
        logit = keep[:, 1, 14 * N:14 * N + 384]
        prob = keep[:, 1, 15 * N:15 * N + 384]
        prob_t = keep[:, 1, 16 * N:16 * N + 384]
        nmax, rowsum, rrow = stats[:, 16:18], stats[:, 18:20], stats[:, 20:22]
        cg_s = early[:, 0, 0:N].rearrange("p (w t c) -> p w t c", w=2, t=T)
        conv_y = early[:, 0, N:N + SEQ]
        wsg = early[:, 0, 2 * N:2 * N + P]
        merged = section(keep, 0, 1)
        part = section(keep, 1, 1)
        x_o = section(keep, 2, 4)
        fg_all = keep[:, 0, 10 * N:14 * N]
        y_out = section(keep, 14, 4)
        ssq = stats[:, 24:32].rearrange("p (t c) -> p t c", t=T)
        var, root, inv, tmp2 = stats[:, 32:34], stats[:, 34:36], stats[:, 36:38], stats[:, 38:40]

        x_loaded = [sem(f"x_loaded{t}") for t in range(T)]
        g_loaded = sem("g_loaded")
        small_loaded = sem("small_loaded")
        raw_loaded = [sem(f"raw_loaded{s}") for s in range(RING)]
        high_split = sem("high_split")
        low_split = sem("low_split")
        sub_used = sem("sub_used")
        tile0_done = sem("tile0_done")
        evac = [sem(f"evac{t}") for t in range(T)]
        sq_done, var_done, root_done = sem("sq_done"), sem("var_done"), sem("root_done")
        norm_step = sem("norm_step")
        xn_ready, xt_done, hh_ready, hl_ready = sem("xn_ready"), sem("xt_done"), sem("hh_ready"), sem("hl_ready")
        ikw_ready, ikt_done, ikt_ready = sem("ikw_ready"), sem("ikt_done"), sem("ikt_ready")
        small_done, small_ready, ws_masked = sem("small_done"), sem("small_ready"), sem("ws_masked")
        table_done, table_ready, table_stored = sem("table_done"), sem("table_ready"), sem("table_stored")
        bias_loaded, bias_done, bias_ready = sem("bias_loaded"), sem("bias_done"), sem("bias_ready")
        iq_ready, iqt_done, iqt_ready = sem("iq_ready"), sem("iqt_done"), sem("iqt_ready")
        index_done, relu_ready, score_step = sem("index_done"), sem("relu_ready"), sem("score_step")
        score_masked, top_step, mask_ready, bias_masked = sem("score_masked"), sem("top_step"), sem("mask_ready"), sem("bias_masked")
        silu_ready, gate_step = sem("silu_ready"), sem("gate_step")
        qk_ready, qkt_done, qkt_ready, logit_done = sem("qk_ready"), sem("qkt_done"), sem("qkt_ready"), sem("logit_done")
        soft_step, prob_ready, probt_done, probt_ready = sem("soft_step"), sem("prob_ready"), sem("probt_done"), sem("probt_ready")
        pv_done, yc_step = sem("pv_done"), sem("yc_step")
        cg_ready, cgt_done, conv_step = sem("cg_ready"), sem("cgt_done"), sem("conv_step")
        wsg_ready, mix_done, ya_ready = sem("wsg_ready"), sem("mix_done"), sem("ya_ready")
        yt_done, yh_ready, yl_ready = sem("yt_done"), sem("yh_ready"), sem("yl_ready")
        sig_ready, merge_step, merge_ready = sem("sig_ready"), sem("merge_step"), sem("merge_ready")
        mt_done, mh_ready, ml_ready = sem("mt_done"), sem("mh_ready"), sem("ml_ready")
        xo_loaded, fg_loaded, ssq_ready = sem("xo_loaded"), sem("fg_loaded"), sem("ssq_ready")
        xo_ready = [sem(f"xo_ready{t}") for t in range(T)]
        xg_ready, inv_ready, stored = sem("xg_ready"), sem("inv_ready"), sem("stored")
        y_ready = [sem(f"y_ready{t}") for t in range(T)]

        block_ = ctx.enter_context(nc.Block())

        @block_.sync
        def _(sp):
            for t in range(T):
                sp.dma_start(x_s[:, t], x_v[:, t]).then_inc(x_loaded[t], 16)
                if t == 0:
                    sp.dma_start(g_all, norm_g.to_broadcast([P, D])).then_inc(g_loaded, 16)

            for n in range(2):
                sp.dma_start(raw[:, n, 0:KW * IKW].rearrange("p (k c) -> p k c", k=KW),
                             w_in_v[:, n * KW:(n + 1) * KW, I_K:I_K + IKW]).then_inc(raw_loaded[n], 16)

            def load(n, slot, k0, weights, col):
                sp.wait_ge(low_split, n - RING + 1)
                sp.dma_start(raw[:, slot].rearrange("p (k c) -> p k c", k=KS),
                             weights[:, k0:k0 + KS, bass.ds(col, N)]).then_inc(raw_loaded[slot], 16)

            for g in range(2):
                sp.dma_start(raw[:, 2 + g].rearrange("p (k c) -> p k c", k=KS),
                             w_in_v[:, KS * g:KS * g + KS, C_Z:C_Z + N]).then_inc(raw_loaded[2 + g], 16)
            for g in range(2, SUB):
                load(SUB1 + g, (SUB1 + g) % RING, KS * g, w_in_v, C_Z)
            for g in range(SUB):
                load(SUB1 + SUB + g, (SUB1 + g) % RING, KS * g, w_in_v, C_Z + N)
            first = SUB1 + 2 * SUB
            for col, count in PHASE1[1:] + PHASE2 + PHASE3 + PHASE4 + PHASE5 + PHASE6 + PHASE7:
                with sp.Fori(0, count) as c:
                    for g in range(SUB):
                        load(first + SUB * c + g, (SUB1 + g) % RING, KS * g, w_in_v, col + N * c)
                first += SUB * count
            with sp.Fori(0, 4) as j:
                for b in range(3):
                    for g in range(SUBP):
                        n = SUBP * b + g
                        load(SUBP0 + 3 * SUBP * j + n, (SUB1 + n) % RING, KS * g, p_v[b], N * j)
            sp.wait_ge(yt_done, 8)
            sp.wait_ge(yl_ready, 12)
            sp.dma_start(x_o, x_v).then_inc(xo_loaded, 16)
            with sp.Fori(0, 4) as j:
                for g in range(SUB):
                    load(SUBO + SUB * j + g, (SUB1 + g) % RING, KS * g, w_o_v, N * j)
            sp.wait_ge(merge_ready, 4 * T)
            sp.dma_start(fg_all, final_g.unsqueeze(0).to_broadcast([P, D])).then_inc(fg_loaded, 16)
            for i in range(2 * T):
                t, half = i % T, slice((i // T) * WIDTH, (i // T + 1) * WIDTH)
                sp.wait_ge(y_ready[t], i // T + 1)
                sp.dma_start(out_v[:, t, half], y_out[:, t, half]).then_inc(stored, 16)
            sp.wait_ge(stored, 16 * 2 * T)

        @block_.gpsimd
        def _(pool):
            pool.dma_start(ident[:], identity).then_inc(small_loaded, 16)
            pool.dma_start(flip_s, flip).then_inc(small_loaded, 16)
            pool.dma_start(onehot, buckets).then_inc(small_loaded, 16)
            pool.dma_start(rel, rel_bias).then_inc(small_loaded, 16)
            pool.dma_start(small[0:KW], a_b[0]).then_inc(small_loaded, 16)
            pool.dma_start(small[KW:KW + TAPS * KW], b_conv[0].rearrange("r (k c) -> (r k) c", c=P)).then_inc(small_loaded, 16)
            pool.dma_start(ws_s.rearrange("p (g s) -> p g s", g=KW), a_ws[0].rearrange("g t s -> t g s")).then_inc(small_loaded, 16)
            pool.wait_ge(table_ready, 1)
            pool.dma_start(table_dram, table).then_inc(table_stored, 16)
            pool.wait_ge(table_stored, 16)
            pool.wait_ge(hl_ready, 2 * KD // 4)
            pool.dma_start(bias_rev.rearrange("p (h s) -> p h s", h=HEADS),
                           bass.AP(table_dram.tensor, 0, [[1, P], [N, HEADS], [1, SEQ]])).then_inc(bias_loaded, 16)
            pool.wait_ge(small_ready, 4)
            pool.affine_select(out=ws_t[:], in_=ws_t[:], compare_op=ALU.is_ge, fill=0.0, base=0,
                               pattern=[[0, KW], [1, P]], channel_multiplier=-1).then_inc(ws_masked, 1)
            pool.wait_ge(score_step, 1 + 4 * HEADS)
            for i, c in enumerate((0, SEQ)):
                pool.affine_select(out=score[:, c:c + P], in_=score[:, c:c + P], compare_op=ALU.is_ge, fill=NEG,
                                   base=0, pattern=[[-1, P]], channel_multiplier=1).then_inc(score_masked, 1)
            pool.wait_ge(mask_ready, 1)
            for c in (0, SEQ):
                pool.affine_select(out=mask[:, c:c + P], in_=mask[:, c:c + P], compare_op=ALU.is_ge, fill=NEG,
                                   base=0, pattern=[[-1, P]], channel_multiplier=1).then_inc(bias_masked, 1)
            pool.wait_ge(bias_masked, 2)
            pool.wait_ge(bias_ready, 4)
            for h in range(HEADS):
                pool.tensor_tensor(bias_m[:, h, 0:P], bias[:, h, P:SEQ], mask[:, 0:P], ALU.add).then_inc(bias_masked, 1)
                pool.tensor_tensor(bias_m[:, h, P:], bias[:, h], mask[:, P:], ALU.add).then_inc(bias_masked, 1)

            pool.wait_ge(fg_loaded, 16)
            for j in range(4):
                for t in range(T):
                    c = slice(j * N, (j + 1) * N)
                    pool.wait_ge(xo_ready[t], j + 1)
                    pool.tensor_tensor(y_out[:, t, c], x_o[:, t, c], fg_all[:, c], ALU.mult).then_inc(xg_ready, 1)

        @block_.scalar
        def _(act):
            def split(n, slot, turn, width=KS * N):
                act.wait_ge(raw_loaded[slot], 16 * (turn + 1))
                act.copy(wh[:, slot, 0:width], raw[:, slot, 0:width]).then_inc(high_split, 1)

            def split_ahead(base, it, per, g):
                act.wait_ge(sub_used, base + per * it + g + 1)
                split(0, (SUB1 + g) % RING, (base - SUB1) // RING + (per // RING) * it + (SUB1 + g) // RING + 1)

            def move(q, dst):
                act.wait_ge(tile0_done, q + 1)
                act.copy(dst, acc[0]).then_inc(evac[0], 1)

            for t in range(T):
                act.wait_ge(x_loaded[t], 16)
                act.activation(xn[:, t], x_s[:, t], ACT.Square, accum_out=ssq[:, t, 0:1]).then_inc(sq_done, 1)
                act.wait_ge(var_done, t + 1)
                act.activation(root[:, t:t + 1], var[:, t:t + 1], ACT.Sqrt).then_inc(root_done, 1)
            for n in range(2):
                split(n, n, 0, KW * IKW)
            for i in range(2 * KD // 4):
                t, k = i // 4, 4 * (i % 4)
                act.wait_ge(xt_done, i + 1)
                act.copy(hh[:, k:k + 4, t * P:(t + 1) * P], blk(bank[i % 6])).then_inc(hh_ready, 1)
            for n in range(2, 4):
                split(n, n, 0)
            act.wait_ge(sub_used, 1)
            split(4, 0, 1)
            act.wait_ge(sub_used, 2)
            act.wait_ge(tile0_done, 1)
            for i in range(2):
                act.copy(ik_s[:, i * IDX_DIM:(i + 1) * IDX_DIM], acc[0][:, 0:IDX_DIM]).then_inc(ikw_ready, 1)
            act.mul(iw[:, 0], acc[0][:, IDX_DIM:IKW], IDX_HEADS ** -0.5 * IDX_DIM ** -0.5).then_inc(evac[0], 1)
            split(5, 1, 1)
            act.wait_ge(small_done, 3)
            act.copy(ab_t[:], bank[2][:, 0:KW]).then_inc(small_ready, 1)
            act.copy(conv_t[:], bank[2][:, KW:KW + TAPS * KW].rearrange("p (r k) -> p r k", r=TAPS)).then_inc(small_ready, 1)
            for i in range(2):
                act.copy(ws_t[:, 4 * i:4 * i + 4], blk(bank[3 + i])).then_inc(small_ready, 1)
            act.wait_ge(table_done, 1)
            act.copy(table, bank[5][0:HEADS]).then_inc(table_ready, 1)
            act.wait_ge(ikt_done, 1)
            act.copy(ik_t[:], bank[0][:, 0:SEQ]).then_inc(ikt_ready, 1)
            with act.Fori(0, 4) as c:
                for g in range(SUB):
                    if g == SUB - 1:
                        move(CH1 + c, chunk(keep, CZ + c, 0))
                    split_ahead(SUB1, c, SUB, g)
            act.wait_ge(bias_done, 1)
            for i in range(4):
                act.copy(keep[:, 0, (8 + i) * N:(9 + i) * N], bank[i]).then_inc(bias_ready, 1)
            with act.Fori(0, 8) as c:
                for g in range(SUB):
                    if g == 0:
                        act.copy(iq_s, block(keep, IQ, c)).then_inc(iq_ready, 1)
                    if g == 2:
                        act.wait_ge(iqt_done, c + 1)
                        act.copy(iq_t, bank[0][:, 0:SEQ]).then_inc(iqt_ready, 1)
                    if g == 4:
                        act.wait_ge(index_done, c + 1)
                        for h in range(2):
                            act.activation(relu[:, h], bank[1 + h][:, 0:384], ACT.Relu).then_inc(relu_ready, 1)
                    if g == SUB - 1:
                        move(CH2 + c, chunk(early, c, 0))
                    split_ahead(SUB2, c, SUB, g)
            for c in range(2):
                for g in range(SUB):
                    if c == 0 and g == 1:
                        act.activation(section(keep, CZ), section(keep, CZ), ACT.Silu).then_inc(silu_ready, 1)
                    if g == SUB - 1:
                        move(CH3 + c, chunk(keep, BC + c, 0))
                    split_ahead(SUB3, c, SUB, g)
            with act.Fori(0, 4) as c:
                for g in range(SUB):
                    if g == SUB - 1:
                        move(CH4 + c, chunk(early, BX + c, 0))
                    split_ahead(SUB4, c, SUB, g)
            act.wait_ge(evac[1], CH5)
            act.wait_ge(evac[0], CH5)
            act.activation(section(early, BZ), section(early, BZ), ACT.Silu).then_inc(silu_ready, 1)
            with act.Fori(0, 8) as c:
                for g in range(SUB):
                    if g == 0:
                        for w, slot in enumerate((Q, K)):
                            act.copy(qk_s[:, w], block(early, slot, c)).then_inc(qk_ready, 1)
                    if g == 2:
                        act.wait_ge(qkt_done, c + 1)
                        act.copy(qk_t, bank[0]).then_inc(qkt_ready, 1)
                    if g == 4:
                        act.wait_ge(soft_step, 4 * c + 4)
                        for i, part_ in enumerate((slice(0, P), slice(P, 384))):
                            act.activation(prob[:, part_], logit[:, part_], ACT.Exp, bias=nmax[:, i:i + 1],
                                           accum_out=rowsum[:, i:i + 1]).then_inc(prob_ready, 1)
                    if g == SUB - 1:
                        move(CH5 + c, chunk(keep, AZ + c, 0))
                    split_ahead(SUB5, c, SUB, g)
            act.wait_ge(evac[1], CH6)
            act.wait_ge(evac[0], CH6)
            act.activation(section(keep, AZ), section(keep, AZ), ACT.Silu).then_inc(silu_ready, 1)
            with act.Fori(0, 8) as c:
                for g in range(SUB):
                    if g == 0:
                        for w, slot in enumerate((BX, BG)):
                            act.copy(cg_s[:, w], block(early, slot, c)).then_inc(cg_ready, 1)
                    if g == 3:
                        act.copy(wsg, ws_t[:, bass.ds(c, 1)].rearrange("p a t -> p (a t)")).then_inc(wsg_ready, 1)
                    if g == SUB - 1:
                        move(CH6 + c, chunk(keep, GC + c, 0))
                    split_ahead(SUB6, c, SUB, g)
            for c in range(2):
                for g in range(SUB):
                    n = SUB * c + g
                    if n % 2:
                        i = n // 2
                        act.wait_ge(yt_done, i + 1)
                        act.copy(yh[:, 2 * i:2 * i + 2], bank[i % 2].rearrange("p (k t) -> p k t", k=2)).then_inc(yh_ready, 1)
                    if n % 4 == 2:
                        k = n // 2 - 1
                        if k == 0:
                            act.wait_ge(conv_step, 4 * KW)
                        act.copy(yh[:, 2 * KW + k:2 * KW + k + 2].rearrange("p k (t c) -> p k t c", t=T),
                                 keep[:, :, YB * N + k * P:YB * N + (k + 2) * P].rearrange("p t (k c) -> p k t c", c=P)
                                 ).then_inc(yh_ready, 1)
                    if g == SUB - 1:
                        move(CH7 + c, chunk(keep, GB + c, 0))
                    split_ahead(SUB7, c, SUB, g)
            act.wait_ge(evac[0], CHP)
            act.wait_ge(evac[1], CHP)
            def high_merged(j, i):
                act.wait_ge(mt_done, 2 * j + i + 1)
                act.copy(hh[:, bass.ds(4 * j + 2 * i, 2)], bank_m[i].rearrange("p (k t) -> p k t", k=2)).then_inc(mh_ready, 1)

            def outputs(j, first):
                for n in range(3 * SUBP):
                    if n % SUBP == 0:
                        gate = (GC, GA, GB)[n // SUBP]
                        here = keep[:, :, bass.ds((gate + j) * N, N)]
                        act.activation(here, here, ACT.Sigmoid).then_inc(sig_ready, 1)
                    if n in (2, 3) and not first:
                        high_merged(j - 1, n - 2)
                    split_ahead(SUBP0, j, 3 * SUBP, n)

            outputs(0, True)
            with act.Fori(1, 4) as j:
                outputs(j, False)

            def squares(j):
                for t in range(T):
                    act.wait_ge(xo_ready[t], j + 1)
                    act.activation(part[:, t], x_o[:, t, bass.ds(j * N, N)], ACT.Square,
                                   accum_out=ssq[:, t, bass.ds(j, 1)]).then_inc(ssq_ready, 1)

            for g in range(SUB):
                if g in (2, 3):
                    high_merged(3, g - 2)
                split_ahead(SUBO, 0, SUB, g)
            with act.Fori(1, 3) as j:
                for g in range(SUB):
                    if g == 1:
                        squares(j - 1)
                    split_ahead(SUBO, j, SUB, g)
            for g in range(SUB - RING):
                if g == 1:
                    squares(2)
                split_ahead(SUBO, 3, SUB, g)
            squares(3)
            act.wait_ge(var_done, T + 1)
            act.activation(root, var, ACT.Sqrt).then_inc(root_done, 1)
            act.wait_ge(xg_ready, 4 * T)
            act.wait_ge(inv_ready, T + 1)
            for i in range(2):
                here = y_out[:, 0, i * WIDTH:(i + 1) * WIDTH]
                act.activation(here, here, ACT.Copy, scale=inv[:, 0:1]).then_inc(y_ready[0], 1)

        @block_.vector
        def _(dve):
            def split(n, slot, width=KS * N):
                dve.wait_ge(high_split, n + 1)
                dve.tensor_tensor(wl[:, slot, 0:width], raw[:, slot, 0:width], wh[:, slot, 0:width].bitcast(F32),
                                  ALU.subtract).then_inc(low_split, 1)

            def split_ahead(base, it, per, g):
                split(base + per * it + g + RING, (SUB1 + g) % RING)

            def move(q, last, dst):
                dve.wait_ge(sub_used, last + 1)
                dve.tensor_copy(dst, acc[1]).then_inc(evac[1], 1)

            steps, invs = [0], [0]

            def rsqrt(cols):
                v, r, i, s = (a[:, cols] for a in (var, root, inv, tmp2))
                for op in (lambda: dve.reciprocal(i, r),
                           lambda: dve.tensor_tensor(s, i, i, ALU.mult),
                           lambda: dve.tensor_tensor(s, s, v, ALU.mult),
                           lambda: dve.tensor_scalar(s, s, -0.5, 1.5, ALU.mult, ALU.add)):
                    op().then_inc(norm_step, 1)
                    steps[0] += 1
                    dve.wait_ge(norm_step, steps[0])
                invs[0] += 1
                dve.tensor_tensor(i, i, s, ALU.mult).then_inc(inv_ready, 1)
                dve.wait_ge(inv_ready, invs[0])

            for t in range(T):
                dve.wait_ge(sq_done, t + 1)
                dve.tensor_scalar(var[:, t:t + 1], ssq[:, t, 0:1], 1.0 / D, EPS, ALU.mult, ALU.add).then_inc(var_done, 1)
                dve.wait_ge(root_done, t + 1)
                dve.wait_ge(var_done, t + 1)
                rsqrt(slice(t, t + 1))
                if t == 0:
                    dve.wait_ge(g_loaded, 16)
                for i in range(4):
                    c = slice(i * N, (i + 1) * N)
                    dve.scalar_tensor_tensor(xn[:, t, c], x_s[:, t, c], inv[:, t:t + 1], g_all[:, c],
                                             ALU.mult, ALU.mult).then_inc(xn_ready, 1)
            for n in range(2):
                split(n, n, KW * IKW)
            for i in range(2 * KD // 4):
                t, k = i // 4, 4 * (i % 4)
                dve.wait_ge(hh_ready, i + 1)
                dve.tensor_tensor(hl[:, k:k + 4, t * P:(t + 1) * P], blk(bank[i % 6]),
                                  hh[:, k:k + 4, t * P:(t + 1) * P].bitcast(F32), ALU.subtract).then_inc(hl_ready, 1)
            for n in range(2, 4):
                split(n, n)
            split(4, 0)
            dve.wait_ge(sub_used, 2)
            for i in range(2):
                dve.tensor_copy(ik_s[:, P + i * IDX_DIM:P + (i + 1) * IDX_DIM], acc[1][:, 0:IDX_DIM]).then_inc(ikw_ready, 1)
            dve.tensor_scalar(iw[:, 1], acc[1][:, IDX_DIM:IKW], IDX_HEADS ** -0.5 * IDX_DIM ** -0.5, None,
                              ALU.mult).then_inc(evac[1], 1)
            split(5, 1)
            dve.memset(score, 0.0).then_inc(score_step, 1)
            with dve.Fori(0, 4) as c:
                for g in range(SUB):
                    if g == SUB - 1:
                        move(0, SUB1 + SUB * c + g, chunk(keep, CZ + c, 1))
                    split_ahead(SUB1, c, SUB, g)
            with dve.Fori(0, 8) as c:
                for g in range(SUB):
                    if g == 5:
                        for h in range(2):
                            dve.wait_ge(relu_ready, 2 * c + h + 1)
                            for t, s in enumerate((slice(0, P), slice(P, 384))):
                                if t == 0:
                                    dve.wait_ge(score_step, 4 * c + 2 * h + 1)
                                dve.scalar_tensor_tensor(score[:, s], relu[:, h, s], iw[:, t, bass.ds(2 * c + h, 1)],
                                                         score[:, s], ALU.mult, ALU.add).then_inc(score_step, 1)
                    if g == SUB - 1:
                        move(0, SUB2 + SUB * c + g, chunk(early, c, 1))
                    split_ahead(SUB2, c, SUB, g)
            for c in range(2):
                for g in range(SUB):
                    n = SUB * c + g
                    t, s = n % 2, (slice(0, P), slice(P, 384))[n % 2]
                    if n == 0:
                        dve.wait_ge(score_masked, 2)
                    if n >= 2:
                        dve.wait_ge(top_step, 2 * (n - 1))
                    dve.max(top8[:, t], score[:, s]).then_inc(top_step, 1)
                    dve.wait_ge(top_step, 2 * n + 1)
                    dve.match_replace(score[:, s], top8[:, t], score[:, s], TAKEN).then_inc(top_step, 1)
                    if g == SUB - 1:
                        move(0, SUB3 + n, chunk(keep, BC + c, 1))
                    split_ahead(SUB3, c, SUB, g)
            dve.wait_ge(top_step, 2 * 2 * TOPK // 8)
            dve.tensor_scalar(mask, score, 0.5 * TAKEN, NEG, ALU.is_gt, ALU.mult).then_inc(mask_ready, 1)
            with dve.Fori(0, 4) as c:
                for g in range(SUB):
                    if g == SUB - 1:
                        move(0, SUB4 + SUB * c + g, chunk(early, BX + c, 1))
                    split_ahead(SUB4, c, SUB, g)
            dve.wait_ge(evac[0], CH5)
            dve.wait_ge(evac[1], CH5)
            dve.tensor_tensor(section(early, BX), section(early, BX), section(keep, BC), ALU.mult).then_inc(gate_step, 1)
            dve.wait_ge(silu_ready, 2)
            dve.tensor_tensor(section(early, BG), section(early, BG), section(early, BZ), ALU.mult).then_inc(gate_step, 1)
            dve.wait_ge(bias_masked, 2 + 2 * HEADS)
            with dve.Fori(0, 8) as c:
                for g in range(SUB):
                    if g == 3:
                        dve.wait_ge(logit_done, c + 1)
                        dve.scalar_tensor_tensor(logit, bank[1][:, 0:384], SCALE,
                                                 bias_m[:, bass.ds(c, 1)].rearrange("p a s -> p (a s)"),
                                                 ALU.mult, ALU.add).then_inc(soft_step, 1)
                        dve.wait_ge(soft_step, 4 * c + 1)
                        dve.reduce_max(tmp2[:, 0:1], logit[:, 0:P], AX_X).then_inc(soft_step, 1)
                        dve.reduce_max(tmp2[:, 1:2], logit[:, P:], AX_X).then_inc(soft_step, 1)
                        dve.wait_ge(soft_step, 4 * c + 3)
                        dve.tensor_scalar(nmax, tmp2, -1.0, None, ALU.mult).then_inc(soft_step, 1)
                    if g == 5:
                        dve.wait_ge(probt_done, c + 1)
                        dve.tensor_copy(prob_t, bank[2][:, 0:384]).then_inc(probt_ready, 1)
                        dve.wait_ge(prob_ready, 2 * c + 2)
                        dve.reciprocal(rrow, rowsum).then_inc(yc_step, 1)
                    if g == 7:
                        dve.wait_ge(pv_done, c + 1)
                        dve.wait_ge(yc_step, 3 * c + 1)
                        for t in range(T):
                            here = keep[:, t, bass.ds(CZ * N + c * P, P)]
                            dve.scalar_tensor_tensor(here, bank[3][:, t * P:(t + 1) * P], rrow[:, t:t + 1], here,
                                                     ALU.mult, ALU.mult).then_inc(yc_step, 1)
                    if g == SUB - 1:
                        move(0, SUB5 + SUB * c + g, chunk(keep, AZ + c, 1))
                    split_ahead(SUB5, c, SUB, g)
            dve.wait_ge(silu_ready, 3)
            dve.tensor_tensor(section(keep, AU), section(keep, AU), section(keep, AZ), ALU.mult).then_inc(gate_step, 1)
            dve.wait_ge(gate_step, 3)
            with dve.Fori(0, 8) as c:
                for g in range(SUB):
                    if g == 2:
                        dve.wait_ge(cgt_done, c + 1)
                        tap = [conv_t[:, r, bass.ds(c, 1)] for r in range(TAPS)]
                        dve.tensor_scalar(conv_y, bank[0][:, 0:SEQ], tap[2], None, ALU.mult).then_inc(conv_step, 1)
                        for r in range(1, TAPS):
                            dve.wait_ge(conv_step, 4 * c + r)
                            dve.scalar_tensor_tensor(conv_y[:, r:], bank[0][:, 0:SEQ - r], tap[2 - r], conv_y[:, r:],
                                                     ALU.mult, ALU.add).then_inc(conv_step, 1)
                        dve.wait_ge(conv_step, 4 * c + 3)
                        dve.tensor_tensor(block(keep, YB, c), conv_y.rearrange("p (t s) -> p t s", t=T),
                                          bank[0][:, SEQ:].rearrange("p (t s) -> p t s", t=T), ALU.mult).then_inc(conv_step, 1)
                    if g == 5:
                        dve.wait_ge(mix_done, c + 1)
                        dve.scalar_tensor_tensor(block(keep, AU, c), bank[1][:, 0:SEQ].rearrange("p (t s) -> p t s", t=T),
                                                 ab_t[:, bass.ds(c, 1)], block(keep, AU, c), ALU.add,
                                                 ALU.mult).then_inc(ya_ready, 1)
                    if g == SUB - 1:
                        move(0, SUB6 + SUB * c + g, chunk(keep, GC + c, 1))
                    split_ahead(SUB6, c, SUB, g)
            dve.wait_ge(conv_step, 4 * KW)
            for c in range(2):
                for g in range(SUB):
                    n = SUB * c + g
                    done = (n + 1) // 2 + (n + 2) // 4
                    if n % 2:
                        i = n // 2
                        dve.wait_ge(yh_ready, done)
                        dve.tensor_tensor(yl[:, 2 * i:2 * i + 2], bank[i % 2].rearrange("p (k t) -> p k t", k=2),
                                          yh[:, 2 * i:2 * i + 2].bitcast(F32), ALU.subtract).then_inc(yl_ready, 1)
                    if n % 4 == 2:
                        k = n // 2 - 1
                        dve.wait_ge(yh_ready, done)
                        dve.tensor_tensor(yl[:, 2 * KW + k:2 * KW + k + 2].rearrange("p k (t c) -> p k t c", t=T),
                                          keep[:, :, YB * N + k * P:YB * N + (k + 2) * P].rearrange("p t (k c) -> p k t c", c=P),
                                          yh[:, 2 * KW + k:2 * KW + k + 2].bitcast(F32).rearrange("p k (t c) -> p k t c", t=T),
                                          ALU.subtract).then_inc(yl_ready, 1)
                    if g == SUB - 1:
                        move(0, SUB7 + n, chunk(keep, GB + c, 1))
                    split_ahead(SUB7, c, SUB, g)
            def low_merged(j, i):
                dve.wait_ge(mh_ready, 2 * j + i + 1)
                here = bass.ds(4 * j + 2 * i, 2)
                dve.tensor_tensor(hl[:, here], bank_m[i].rearrange("p (k t) -> p k t", k=2), hh[:, here].bitcast(F32),
                                  ALU.subtract).then_inc(ml_ready, 1)

            def outputs(j, first):
                for n in range(3 * SUBP):
                    if n in (2, 3) and not first:
                        low_merged(j - 1, n - 2)
                    if n % SUBP == SUBP - 1:
                        b = n // SUBP
                        gate = (GC, GA, GB)[b]
                        dst = merged if b == 0 else part
                        dve.wait_ge(sig_ready, 3 * j + b + 1)
                        dve.wait_ge(tile0_done, CHP + 3 * j + b + 1)
                        dve.tensor_tensor(dst[:, 0], acc_p[b][0], keep[:, 0, bass.ds((gate + j) * N, N)], ALU.mult).then_inc(evac[0], 1)
                        dve.wait_ge(sub_used, SUBP0 + 3 * SUBP * j + n + 1)
                        dve.tensor_tensor(dst[:, 1], acc_p[b][1], keep[:, 1, bass.ds((gate + j) * N, N)], ALU.mult).then_inc(evac[1], 1)
                        for t in range(T if b else 0):
                            dve.wait_ge(evac[t], CHP + 3 * j + b + 1)
                            if b == 2:
                                dve.wait_ge(merge_step, T * j + t + 1)
                            dve.tensor_tensor(merged[:, t], merged[:, t], part[:, t],
                                              ALU.add).then_inc(merge_step if b == 1 else merge_ready, 1)
                    split_ahead(SUBP0, j, 3 * SUBP, n)

            outputs(0, True)
            with dve.Fori(1, 4) as j:
                outputs(j, False)

            def residual(j, t):
                here = x_o[:, t, bass.ds(j * N, N)]
                dve.tensor_tensor(here, psum[:, bass.ds(T * j + t, 1)].rearrange("p a n -> p (a n)"), here,
                                  ALU.add).then_inc(xo_ready[t], 1)

            dve.wait_ge(xo_loaded, 16)
            for g in range(SUB):
                if g in (2, 3):
                    low_merged(3, g - 2)
                split_ahead(SUBO, 0, SUB, g)
            with dve.Fori(1, 3) as j:
                for g in range(SUB):
                    if g == 0:
                        dve.wait_ge(sub_used, SUBO + SUB * j)
                        for t in range(T):
                            residual(j - 1, t)
                    split_ahead(SUBO, j, SUB, g)
            for g in range(SUB - RING):
                if g == 0:
                    dve.wait_ge(sub_used, SUBO + SUB * 3)
                    for t in range(T):
                        residual(2, t)
                split_ahead(SUBO, 3, SUB, g)
            dve.wait_ge(tile0_done, CHO + 4)
            residual(3, 0)
            dve.wait_ge(sub_used, SUBO + SUB * 4)
            residual(3, 1)
            dve.wait_ge(ssq_ready, T * 4)
            dve.reduce_sum(tmp2, ssq, AX_X).then_inc(norm_step, 1)
            steps[0] += 1
            dve.wait_ge(norm_step, steps[0])
            dve.tensor_scalar(var, tmp2, 1.0 / D, EPS, ALU.mult, ALU.add).then_inc(var_done, 1)
            dve.wait_ge(root_done, T + 1)
            dve.wait_ge(var_done, T + 1)
            rsqrt(slice(0, T))
            dve.wait_ge(xg_ready, 4 * T)
            for i in range(2):
                here = y_out[:, 1, i * WIDTH:(i + 1) * WIDTH]
                dve.tensor_scalar(here, here, inv[:, 1:2], None, ALU.mult).then_inc(y_ready[1], 1)

        @block_.tensor
        def _(pe):
            def product(n, slot, g, last, high, low, k0, q, width=N, ks=KS, free=None, dst=acc):
                pe.wait_ge(low_split, n + 1)
                w_h, w_l = (w[:, slot, 0:ks * width].rearrange("p (k c) -> p k c", k=ks) for w in (wh, wl))
                for t in range(T):
                    tok = slice(t * P, (t + 1) * P)
                    if g == 0 and free is not None:
                        pe.wait_ge(free[t], q)
                    for j in range(ks):
                        h, l = high[:, k0 + j, tok], low[:, k0 + j, tok]
                        start, stop = g == 0 and j == 0, last and j == ks - 1
                        to = dst[t][:, 0:width]
                        pe.matmul(to, h, w_h[:, j], start=start, stop=False)
                        pe.matmul(to, h, w_l[:, j], start=False, stop=False)
                        mm = pe.matmul(to, l, w_h[:, j], start=False, stop=stop)
                    if last and t == 0:
                        mm.then_inc(tile0_done, 1)
                mm.then_inc(sub_used, 1)

            def transpose(dst, src):
                return pe.transpose(dst, src, ident[:])

            pe.wait_ge(small_loaded, 16 * 7)
            for i in range(2 * KD // 4):
                t, k = i // 4, 4 * (i % 4)
                pe.wait_ge(xn_ready, i + 1)
                if i >= 6:
                    pe.wait_ge(hl_ready, i - 5)
                for j in range(4):
                    mm = transpose(bank[i % 6][:, j * P:(j + 1) * P], xn[:, t, (k + j) * P:(k + j + 1) * P])
                mm.then_inc(xt_done, 1)
            pe.wait_ge(hl_ready, 2 * KD // 4)
            for n in range(2):
                product(n, n, n, n == 1, hh, hl, n * KW, 0, width=IKW, ks=KW)
            some = KW + TAPS * KW
            pe.transpose(bank[2][:, 0:some], small[0:some], ident[0:some, 0:some]).then_inc(small_done, 1)
            for i in range(2):
                for j in range(4):
                    mm = transpose(bank[3 + i][:, j * P:(j + 1) * P], ws_s[:, (4 * i + j) * P:(4 * i + j + 1) * P])
                mm.then_inc(small_done, 1)
            pe.matmul(bank[5][0:HEADS], rel, onehot, start=True, stop=True).then_inc(table_done, 1)
            pe.wait_ge(ikw_ready, 4)
            for t in range(T):
                mm = transpose(bank[0][:, t * P:(t + 1) * P], ik_s[:, t * P:(t + 1) * P])
            mm.then_inc(ikt_done, 1)
            with pe.Fori(0, 4) as c:
                for g in range(SUB):
                    product(SUB1 + SUB * c + g, (SUB1 + g) % RING, g, g == SUB - 1, hh, hl, KS * g, CH1 + c, free=evac)
            pe.wait_ge(bias_loaded, 16)
            pe.wait_ge(ikt_ready, 1)
            for i in range(4):
                mm = pe.matmul(bank[i], flip_s, bias_rev[:, i * N:(i + 1) * N], start=True, stop=True)
            mm.then_inc(bias_done, 1)
            with pe.Fori(0, 8) as c:
                for g in range(SUB):
                    product(SUB2 + SUB * c + g, (SUB1 + g) % RING, g, g == SUB - 1, hh, hl, KS * g, CH2 + c, free=evac)
                    if g == 1:
                        pe.wait_ge(bias_ready, 4)
                        pe.wait_ge(iq_ready, c + 1)
                        for t in range(T):
                            mm = transpose(bank[0][:, t * P:(t + 1) * P], iq_s[:, t])
                        mm.then_inc(iqt_done, 1)
                    if g == 3:
                        pe.wait_ge(iqt_ready, c + 1)
                        for h in range(2):
                            half = slice(h * IDX_DIM, (h + 1) * IDX_DIM)
                            pe.matmul(bank[1 + h][:, 0:P], iq_t[half, 0:P], ik_t[half, 0:P], start=True, stop=True)
                            mm = pe.matmul(bank[1 + h][:, P:384], iq_t[half, P:SEQ], ik_t[half], start=True, stop=True)
                        mm.then_inc(index_done, 1)
            for c in range(2):
                for g in range(SUB):
                    product(SUB3 + SUB * c + g, (SUB1 + g) % RING, g, g == SUB - 1, hh, hl, KS * g, CH3 + c, free=evac)
            with pe.Fori(0, 4) as c:
                for g in range(SUB):
                    product(SUB4 + SUB * c + g, (SUB1 + g) % RING, g, g == SUB - 1, hh, hl, KS * g, CH4 + c, free=evac)
            with pe.Fori(0, 8) as c:
                for g in range(SUB):
                    product(SUB5 + SUB * c + g, (SUB1 + g) % RING, g, g == SUB - 1, hh, hl, KS * g, CH5 + c, free=evac)
                    if g == 1:
                        pe.wait_ge(qk_ready, 2 * c + 2)
                        for w in range(2):
                            for t in range(T):
                                mm = transpose(bank[0][:, (2 * w + t) * P:(2 * w + t + 1) * P], qk_s[:, w, t])
                        mm.then_inc(qkt_done, 1)
                    if g == 2:
                        pe.wait_ge(qkt_ready, c + 1)
                        pe.matmul(bank[1][:, 0:P], qk_t[:, 0:P], qk_t[:, SEQ:SEQ + P], start=True, stop=True)
                        pe.matmul(bank[1][:, P:384], qk_t[:, P:SEQ], qk_t[:, SEQ:], start=True,
                                  stop=True).then_inc(logit_done, 1)
                    if g == 4:
                        pe.wait_ge(prob_ready, 2 * c + 2)
                        for i in range(3):
                            mm = transpose(bank[2][:, i * P:(i + 1) * P], prob[:, i * P:(i + 1) * P])
                        mm.then_inc(probt_done, 1)
                    if g == 6:
                        pe.wait_ge(probt_ready, c + 1)
                        v = [early[:, t, bass.ds(V * N + c * P, P)] for t in range(T)]
                        pe.matmul(bank[3][:, 0:P], prob_t[:, 0:P], v[0], start=True, stop=True)
                        pe.matmul(bank[3][:, P:SEQ], prob_t[:, P:SEQ], v[0], start=True, stop=False)
                        pe.matmul(bank[3][:, P:SEQ], prob_t[:, SEQ:384], v[1], start=False,
                                  stop=True).then_inc(pv_done, 1)
            with pe.Fori(0, 8) as c:
                for g in range(SUB):
                    product(SUB6 + SUB * c + g, (SUB1 + g) % RING, g, g == SUB - 1, hh, hl, KS * g, CH6 + c, free=evac)
                    if g == 1:
                        pe.wait_ge(cg_ready, 2 * c + 2)
                        for w in range(2):
                            for t in range(T):
                                mm = transpose(bank[0][:, (2 * w + t) * P:(2 * w + t + 1) * P], cg_s[:, w, t])
                        mm.then_inc(cgt_done, 1)
                    if g == 3:
                        pe.wait_ge(wsg_ready, c + 1)
                        pe.matmul(bank[1][:, 0:SEQ], wsg, block(keep, AV, c), start=True, stop=True).then_inc(mix_done, 1)
            pe.wait_ge(ya_ready, KW)
            for c in range(2):
                for g in range(SUB):
                    n = SUB * c + g
                    product(SUB7 + n, (SUB1 + g) % RING, g, g == SUB - 1, hh, hl, KS * g, CH7 + c, free=evac)
                    if n % 2 == 0:
                        i = n // 2
                        slot, k = (CZ, AU)[i // 4], 2 * (i % 4)
                        if i >= 2:
                            pe.wait_ge(yl_ready, yl_after(i - 2))
                        for j in range(2):
                            for t in range(T):
                                mm = transpose(bank[i % 2][:, (2 * j + t) * P:(2 * j + t + 1) * P],
                                               keep[:, t, slot * N + (k + j) * P:slot * N + (k + j + 1) * P])
                        mm.then_inc(yt_done, 1)
            def transpose_merged(j):
                pe.wait_ge(merge_ready, T * j + T)
                for i in range(2):
                    for k in range(2):
                        for t in range(T):
                            mm = transpose(bank_m[i][:, (2 * k + t) * P:(2 * k + t + 1) * P],
                                           merged[:, t, (2 * i + k) * P:(2 * i + k + 1) * P])
                    mm.then_inc(mt_done, 1)

            def outputs(j, first):
                for n in range(3 * SUBP):
                    b, g = n // SUBP, n % SUBP
                    free = evac if b == 0 or not first else None
                    product(SUBP0 + 3 * SUBP * j + n, (SUB1 + n) % RING, g, g == SUBP - 1, yh, yl,
                            b * KW + KS * g, CHP + 3 * j + b - (0 if first else 2), free=free, dst=acc_p[b])
                    if n == 1 and not first:
                        transpose_merged(j - 1)

            pe.wait_ge(yl_ready, 12)
            outputs(0, True)
            with pe.Fori(1, 4) as j:
                outputs(j, False)

            def acc_o(j):
                return [psum[:, bass.ds(T * j + t, 1)].rearrange("p a n -> p (a n)") for t in range(T)]

            pe.wait_ge(ml_ready, 6)
            for g in range(SUB):
                if g == SUB - 2:
                    pe.wait_ge(ml_ready, 8)
                product(SUBO + g, (SUB1 + g) % RING, g, g == SUB - 1, hh, hl, KS * g, CHO - 2, free=evac, dst=acc_o(0))
                if g == 1:
                    transpose_merged(3)
            with pe.Fori(1, 4) as j:
                for g in range(SUB):
                    product(SUBO + SUB * j + g, (SUB1 + g) % RING, g, g == SUB - 1, hh, hl, KS * g, 0, dst=acc_o(j))


def yl_after(i):
    n = 2 * i + 1
    return (n + 1) // 2 + (n + 2) // 4


_INS = ['x', 'norm_g', 'w_in', 'a_ws', 'a_b', 'b_conv', 'p_a', 'p_b', 'p_c', 'w_o', 'rel_bias', 'final_g']


def _constants():
    import numpy as np
    eye = np.eye(P, dtype=np.float32)
    dist = np.maximum(SEQ - 1 - np.arange(N), 0)
    exact = BUCKETS // 2
    large = exact + (np.log(np.maximum(dist, 1) / exact) / np.log(MAX_DISTANCE / exact) * (BUCKETS - exact)).astype(np.int64)
    bucket = np.where(dist < exact, dist, np.minimum(large, BUCKETS - 1))
    onehot = (np.arange(BUCKETS)[:, None] == bucket[None]).astype(np.float32)
    return {"identity": eye, "flip": np.ascontiguousarray(eye[::-1]), "buckets": onehot}


def kernel(**inputs):
    import numpy as np
    import concourse.bacc as bacc
    from concourse.bass_utils import run_bass_kernel_spmd

    nc = bacc.Bacc("TRN2", target_bir_lowering=False, num_devices=1)
    arrays = {name: np.ascontiguousarray(inputs[name]) for name in _INS}
    arrays.update(_constants())
    args = [nc.dram_tensor(name, a.shape, F32, kind="ExternalInput").ap() for name, a in arrays.items()]
    out = nc.dram_tensor("out", (1, SEQ, D), F32, kind="ExternalOutput").ap()
    trunk(nc, *args, out)
    r = run_bass_kernel_spmd(nc, [arrays], core_ids=[0])
    return r.results[0]["out"]
```

```python
from contextlib import ExitStack

import concourse.bass as bass
from concourse import mybir

F32 = mybir.dt.float32
F32R = mybir.dt.float32r
ACT = mybir.ActivationFunctionType
ALU = mybir.AluOpType
AX_X = mybir.AxisListType.X

P = 128
SEQ = 256
D = 2048
T = SEQ // P
KD = D // P
WIDTH = 1024
KW = WIDTH // P
HEADS = 8
IDX_HEADS = 16
IDX_DIM = 64
TOPK = 64
BUCKETS = 32
MAX_DISTANCE = 128
TAPS = 3
EPS = 1e-6
NEG = -1e30
TAKEN = -3e38
SCALE = float(P) ** -0.5
WARM_UP = 18

N = 512
RING = 4
KS = 2
SUB = KD // KS
SUBP = KW // KS

A_U, A_V, A_Z = 0, 1024, 2048
B_G, B_C, B_X, B_Z = 3072, 4096, 5120, 6144
C_Q, C_K, C_V, C_Z = 7168, 8192, 9216, 10240
I_Q, I_K = 11264, 12288
G_A, G_B, G_C = 12368, 14416, 16464
IKW = IDX_DIM + IDX_HEADS

PHASE1 = [(C_Z, 2), (I_Q, 2)]
PHASE2 = [(C_Q, 6), (B_G, 2)]
PHASE3 = [(B_C, 2)]
PHASE4 = [(B_X, 4)]
PHASE5 = [(A_Z, 2), (A_U, 4), (G_B + 2 * N, 2)]
PHASE6 = [(G_C, 4), (G_A, 4)]
PHASE7 = [(G_B, 2)]

SUB1 = 2
SUB2 = SUB1 + 4 * SUB
SUB3 = SUB2 + 8 * SUB
SUB4 = SUB3 + 2 * SUB
SUB5 = SUB4 + 4 * SUB
SUB6 = SUB5 + 8 * SUB
SUB7 = SUB6 + 8 * SUB
SUBP0 = SUB7 + 2 * SUB
SUBO = SUBP0 + 4 * 3 * SUBP
CH1, CH2, CH3, CH4, CH5, CH6, CH7, CHP, CHO = 1, 5, 13, 15, 19, 27, 35, 37, 49

Q, K, V, BG, BX, BZ = 0, 2, 4, 6, 8, 10
EARLY = 12
CZ, IQ, BC, AZ, YB, AU, AV, GB, GC, GA = 0, 2, 2, 2, 2, 4, 6, 6, 10, 14
KEEP = 18


def trunk(nc, x, norm_g, w_in, a_ws, a_b, b_conv, p_a, p_b, p_c, w_o, rel_bias, final_g,
          identity, flip, buckets, out):
    table_dram = nc.dram_tensor("bias_table", (HEADS, N), F32).ap()
    rows = lambda w: w.rearrange("(k p) n -> p k n", p=P)
    w_in_v, w_o_v = rows(w_in[0]), rows(w_o[0])
    p_v = [rows(p_c[0]), rows(p_a[0]), rows(p_b[0])]
    x_v = x[0].rearrange("(t p) d -> p t d", p=P)
    out_v = out[0].rearrange("(t p) d -> p t d", p=P)

    with ExitStack() as ctx:
        def sb(name, shape, dt=F32):
            return ctx.enter_context(nc.sbuf_tensor(name, shape, dt))

        def sem(name):
            return ctx.enter_context(nc.semaphore(name))

        raw = sb("raw", [P, RING, KS * N])
        wh = sb("wh", [P, RING, KS * N], F32R)
        wl = sb("wl", [P, RING, KS * N], F32R)
        hh = sb("hh", [P, KD, SEQ], F32R)
        hl = sb("hl", [P, KD, SEQ], F32R)
        guard = nc.sbuf_tensor("early", [P, T, EARLY * N], F32)
        early = guard.__enter__()
        guard.__exit__(None, None, None)
        yh = sb("yh", [P, 3 * KW, SEQ], F32R)
        yl = sb("yl", [P, 3 * KW, SEQ], F32R)
        keep = sb("keep", [P, T, KEEP * N])
        ws_t = sb("ws_t", [P, KW, P])
        ident = sb("ident", [P, P])
        ik_t = sb("ik_t", [P, SEQ])
        iw = sb("iw", [P, T, IDX_HEADS])
        ab_t = sb("ab_t", [P, KW])
        conv_t = sb("conv_t", [P, TAPS, KW])
        stats = sb("stats", [P, 48])
        psum = ctx.enter_context(nc.psum_tensor("psum", [P, 8, N], F32))
        acc = [psum[:, t] for t in range(T)]
        bank = [psum[:, 2 + i] for i in range(6)]
        acc_p = [[psum[:, T * b + t] for t in range(T)] for b in range(3)]
        bank_m = [psum[:, 6 + i] for i in range(2)]

        def section(buf, slot, n=2):
            return buf[:, :, slot * N:(slot + n) * N]

        def chunk(buf, slot, t):
            return buf[:, t, bass.ds(slot * N, N)]

        def block(buf, slot, i):
            return buf[:, :, bass.ds(slot * N + i * P, P)]

        def blk(ap):
            return ap.rearrange("p (a c) -> p a c", c=P)

        x_s = section(keep, 4, 4)
        squared = section(keep, 0, 4)
        xn = section(keep, 12, 4)
        g_s = early[0:KD, 1, N:N + P]
        g_t = early[:, 1, 2 * N:2 * N + KD]
        one = early[:, 1, 3 * N:3 * N + 1]
        one_root = early[:, 1, 3 * N + 1:3 * N + 2]
        ikw_acc = psum[0:IKW, 0, 0:SEQ]
        x_t = psum[:].rearrange("p b (k t) -> p (b k) t", k=2)
        ws_s = early[:, 0, 0:KW * P]
        small = early[:, 0, 2048:2048 + P]
        onehot = early[0:BUCKETS, 0, 2560:2560 + N]
        rel = early[0:BUCKETS, 0, 3072:3072 + HEADS]
        table = early[0:HEADS, 0, 3584:3584 + N]
        flip_s = early[:, 0, 4096:4096 + P]
        iw_s = early[IDX_DIM:IKW, 0, 4608:4608 + SEQ]
        bias_rev = keep[:, 1, 8 * N:12 * N]
        bias = keep[:, 0, 8 * N:12 * N].rearrange("p (h s) -> p h s", h=HEADS)
        bias_m = keep[:, 0, 12 * N:18 * N].rearrange("p (h s) -> p h s", h=HEADS)
        score = keep[:, 0, 4 * N:4 * N + 384]
        relu = keep[:, 0, 5 * N:5 * N + 768].rearrange("p (h s) -> p h s", h=2)
        iq_s = keep[:, 1, 4 * N:4 * N + SEQ].rearrange("p (t c) -> p t c", t=T)
        iq_t = keep[:, 1, 5 * N:5 * N + SEQ]
        mask = keep[:, 1, 6 * N:6 * N + 384]
        top8 = stats[:, 0:16].rearrange("p (b c) -> p b c", b=2)
        qk_s = keep[:, 1, 12 * N:13 * N].rearrange("p (w t c) -> p w t c", w=2, t=T)
        qk_t = keep[:, 1, 13 * N:14 * N]
        logit = keep[:, 1, 14 * N:14 * N + 384]
        prob = keep[:, 1, 15 * N:15 * N + 384]
        prob_t = keep[:, 1, 16 * N:16 * N + 384]
        nmax, rowsum, rrow = stats[:, 16:18], stats[:, 18:20], stats[:, 20:22]
        cg_s = early[:, 0, 0:N].rearrange("p (w t c) -> p w t c", w=2, t=T)
        conv_y = early[:, 0, N:N + SEQ]
        wsg = early[:, 0, 2 * N:2 * N + P]
        merged = section(keep, 0, 1)
        part = section(keep, 1, 1)
        x_o = section(keep, 2, 4)
        fg_all = keep[:, 0, 10 * N:14 * N]
        y_out = section(keep, 14, 4)
        ssq = stats[:, 24:32].rearrange("p (t c) -> p t c", t=T)
        var, root, inv, tmp2 = stats[:, 32:34], stats[:, 34:36], stats[:, 36:38], stats[:, 38:40]
        partial, inv_root = stats[:, 40:42], stats[:, 42:43]

        x_loaded = [sem(f"x_loaded{i}") for i in range(2 * T)]
        g_loaded = sem("g_loaded")
        ident_loaded, small_loaded = sem("ident_loaded"), sem("small_loaded")
        raw_loaded = [sem(f"raw_loaded{s}") for s in range(RING)]
        high_split = sem("high_split")
        low_split = sem("low_split")
        sub_used = sem("sub_used")
        tile0_done = sem("tile0_done")
        evac = [sem(f"evac{t}") for t in range(T)]
        sq_done, var_done, root_done = sem("sq_done"), sem("var_done"), sem("root_done")
        norm_step = sem("norm_step")
        const_ready, gt_done, gt_ready, xn_ready = sem("const_ready"), sem("gt_done"), sem("gt_ready"), sem("xn_ready")
        xt_done, hh_ready, hl_ready = sem("xt_done"), sem("hh_ready"), sem("hl_ready")
        iws_ready, iwt_done, iw_ready = sem("iws_ready"), sem("iwt_done"), sem("iw_ready")
        small_done, small_ready, ws_masked = sem("small_done"), sem("small_ready"), sem("ws_masked")
        table_done, table_ready, table_stored = sem("table_done"), sem("table_ready"), sem("table_stored")
        bias_loaded, bias_done, bias_ready = sem("bias_loaded"), sem("bias_done"), sem("bias_ready")
        iq_ready, iqt_done, iqt_ready = sem("iq_ready"), sem("iqt_done"), sem("iqt_ready")
        index_done, relu_ready, score_step = sem("index_done"), sem("relu_ready"), sem("score_step")
        score_masked, top_step, mask_ready, bias_masked = sem("score_masked"), sem("top_step"), sem("mask_ready"), sem("bias_masked")
        silu_ready, gate_step = sem("silu_ready"), sem("gate_step")
        qk_ready, qkt_done, qkt_ready, logit_done = sem("qk_ready"), sem("qkt_done"), sem("qkt_ready"), sem("logit_done")
        soft_step, prob_ready, probt_done, probt_ready = sem("soft_step"), sem("prob_ready"), sem("probt_done"), sem("probt_ready")
        pv_done, yc_step = sem("pv_done"), sem("yc_step")
        cg_ready, cgt_done, conv_step = sem("cg_ready"), sem("cgt_done"), sem("conv_step")
        wsg_ready, mix_done, ya_ready = sem("wsg_ready"), sem("mix_done"), sem("ya_ready")
        yt_done, yh_ready, yl_ready = sem("yt_done"), sem("yh_ready"), sem("yl_ready")
        sig_ready, merge_step, merge_ready = sem("sig_ready"), sem("merge_step"), sem("merge_ready")
        mt_done, mh_ready, ml_ready = sem("mt_done"), sem("mh_ready"), sem("ml_ready")
        xo_loaded, fg_loaded, ssq_ready = sem("xo_loaded"), sem("fg_loaded"), sem("ssq_ready")
        xo_ready = [sem(f"xo_ready{t}") for t in range(T)]
        xf_ready, inv_ready, stored = sem("xf_ready"), sem("inv_ready"), sem("stored")
        y_ready = [sem(f"y_ready{n}") for n in ("_vector", "_scalar")]

        block_ = ctx.enter_context(nc.Block())

        @block_.sync
        def _(sp):
            for i in range(2 * T):
                t, half = i // 2, slice((i % 2) * WIDTH, (i % 2 + 1) * WIDTH)
                sp.dma_start(x_s[:, t, half], x_v[:, t, half]).then_inc(x_loaded[i], 16)

            for n in range(2):
                sp.dma_start(raw[:, n, 0:KW * IKW].rearrange("p (k c) -> p k c", k=KW),
                             w_in_v[:, n * KW:(n + 1) * KW, I_K:I_K + IKW]).then_inc(raw_loaded[n], 16)

            def load(n, slot, k0, weights, col):
                sp.wait_ge(low_split, n - RING + 1)
                sp.dma_start(raw[:, slot].rearrange("p (k c) -> p k c", k=KS),
                             weights[:, k0:k0 + KS, bass.ds(col, N)]).then_inc(raw_loaded[slot], 16)

            for g in range(2):
                sp.dma_start(raw[:, 2 + g].rearrange("p (k c) -> p k c", k=KS),
                             w_in_v[:, KS * g:KS * g + KS, C_Z:C_Z + N]).then_inc(raw_loaded[2 + g], 16)
            for g in range(2, SUB):
                load(SUB1 + g, (SUB1 + g) % RING, KS * g, w_in_v, C_Z)
            for g in range(SUB):
                load(SUB1 + SUB + g, (SUB1 + g) % RING, KS * g, w_in_v, C_Z + N)
            first = SUB1 + 2 * SUB
            for col, count in PHASE1[1:] + PHASE2 + PHASE3 + PHASE4 + PHASE5 + PHASE6 + PHASE7:
                with sp.Fori(0, count) as c:
                    for g in range(SUB):
                        load(first + SUB * c + g, (SUB1 + g) % RING, KS * g, w_in_v, col + N * c)
                first += SUB * count
            with sp.Fori(0, 4) as j:
                for b in range(3):
                    for g in range(SUBP):
                        n = SUBP * b + g
                        load(SUBP0 + 3 * SUBP * j + n, (SUB1 + n) % RING, KS * g, p_v[b], N * j)
            sp.wait_ge(yt_done, 8)
            sp.wait_ge(yl_ready, 12)
            sp.dma_start(x_o, x_v).then_inc(xo_loaded, 16)
            with sp.Fori(0, 4) as j:
                for g in range(SUB):
                    load(SUBO + SUB * j + g, (SUB1 + g) % RING, KS * g, w_o_v, N * j)
            sp.wait_ge(merge_ready, 4 * T)
            sp.dma_start(fg_all, final_g.unsqueeze(0).to_broadcast([P, D])).then_inc(fg_loaded, 16)
            for i in range(2):
                half = slice(i * WIDTH, (i + 1) * WIDTH)
                sp.wait_ge(y_ready[0], 2 * i + 2)
                sp.dma_start(out_v[:, 0, half], y_out[:, 0, half]).then_inc(stored, 16)
            for i in range(4):
                c = slice(i * N, (i + 1) * N)
                sp.wait_ge(y_ready[i % 2], i // 2 + 1 if i % 2 else 4 + i // 2 + 1)
                sp.dma_start(out_v[:, 1, c], y_out[:, 1, c]).then_inc(stored, 16)
            sp.wait_ge(stored, 16 * 6)

        @block_.gpsimd
        def _(pool):
            pool.dma_start(rel, rel_bias).then_inc(small_loaded, 16)
            pool.dma_start(small[0:KW], a_b[0]).then_inc(small_loaded, 16)
            pool.dma_start(small[KW:KW + TAPS * KW], b_conv[0].rearrange("r (k c) -> (r k) c", c=P)).then_inc(small_loaded, 16)
            pool.dma_start(onehot, buckets).then_inc(small_loaded, 16)
            pool.dma_start(flip_s, flip).then_inc(small_loaded, 16)
            pool.dma_start(ws_s.rearrange("p (g s) -> p g s", g=KW), a_ws[0].rearrange("g t s -> t g s")).then_inc(small_loaded, 16)
            pool.wait_ge(table_ready, 1)
            pool.dma_start(table_dram, table).then_inc(table_stored, 16)
            pool.wait_ge(table_stored, 16)
            pool.dma_start(bias_rev.rearrange("p (h s) -> p h s", h=HEADS),
                           bass.AP(table_dram.tensor, 0, [[1, P], [N, HEADS], [1, SEQ]])).then_inc(bias_loaded, 16)
            pool.wait_ge(small_ready, 4)
            pool.affine_select(out=ws_t[:], in_=ws_t[:], compare_op=ALU.is_ge, fill=0.0, base=0,
                               pattern=[[0, KW], [1, P]], channel_multiplier=-1).then_inc(ws_masked, 1)
            pool.wait_ge(score_step, 1 + 4 * HEADS)
            for i, c in enumerate((0, SEQ)):
                pool.affine_select(out=score[:, c:c + P], in_=score[:, c:c + P], compare_op=ALU.is_ge, fill=NEG,
                                   base=0, pattern=[[-1, P]], channel_multiplier=1).then_inc(score_masked, 1)
            pool.wait_ge(mask_ready, 1)
            for c in (0, SEQ):
                pool.affine_select(out=mask[:, c:c + P], in_=mask[:, c:c + P], compare_op=ALU.is_ge, fill=NEG,
                                   base=0, pattern=[[-1, P]], channel_multiplier=1).then_inc(bias_masked, 1)
            pool.wait_ge(bias_masked, 2)
            pool.wait_ge(bias_ready, 4)
            for h in range(HEADS):
                pool.tensor_tensor(bias_m[:, h, 0:P], bias[:, h, P:SEQ], mask[:, 0:P], ALU.add).then_inc(bias_masked, 1)
                pool.tensor_tensor(bias_m[:, h, P:], bias[:, h], mask[:, P:], ALU.add).then_inc(bias_masked, 1)

            pool.wait_ge(fg_loaded, 16)
            for j in range(4):
                for t in range(T):
                    c = slice(j * N, (j + 1) * N)
                    pool.wait_ge(xo_ready[t], j + 1)
                    pool.tensor_tensor(y_out[:, t, c], x_o[:, t, c], fg_all[:, c], ALU.mult).then_inc(xf_ready, 1)

        @block_.scalar
        def _(act):
            def split(n, slot, turn, width=KS * N):
                act.wait_ge(raw_loaded[slot], 16 * (turn + 1))
                act.copy(wh[:, slot, 0:width], raw[:, slot, 0:width]).then_inc(high_split, 1)

            def split_ahead(base, it, per, g):
                act.wait_ge(sub_used, base + per * it + g + 1)
                split(0, (SUB1 + g) % RING, (base - SUB1) // RING + (per // RING) * it + (SUB1 + g) // RING + 1)

            def move(q, dst):
                act.wait_ge(tile0_done, q)
                act.copy(dst, acc[0]).then_inc(evac[0], 1)

            act.dma_start(ident[:], identity).then_inc(ident_loaded, 16)
            act.dma_start(g_s, norm_g.rearrange("o (k c) -> (o k) c", c=P)).then_inc(g_loaded, 16)
            act.wait_ge(const_ready, 1)
            act.activation(one_root, one, ACT.Sqrt)
            def root_of(t):
                act.wait_ge(var_done, 2 * t + 2)
                act.activation(root[:, t:t + 1], var[:, t:t + 1], ACT.Sqrt).then_inc(root_done, 1)

            for t in range(T):
                for i in range(2):
                    act.wait_ge(x_loaded[2 * t + i], 16)
                    half = slice(i * WIDTH, (i + 1) * WIDTH)
                    act.activation(squared[:, t, half], x_s[:, t, half], ACT.Square,
                                   accum_out=ssq[:, t, i:i + 1]).then_inc(sq_done, 1)
                if t == 0:
                    root_of(0)
                    act.wait_ge(gt_done, 1)
                    act.copy(g_t, bank[5][:, 0:KD]).then_inc(gt_ready, 1)
            root_of(1)
            act.wait_ge(gt_ready, 1)
            for k in range(KD):
                if k in (0, KD // 2):
                    n = k // (KD // 2)
                    split(n, n, 0, KW * IKW)
                if k % 2 == 0:
                    act.wait_ge(xt_done, k // 2 + 1)
                act.activation(hh[:, k], x_t[:, k], ACT.Copy, scale=g_t[:, k:k + 1]).then_inc(hh_ready, 1)
            for n in range(2, 4):
                split(n, n, 0)
            act.wait_ge(sub_used, 1)
            split(4, 0, 1)
            act.wait_ge(sub_used, 2)
            act.mul(iw_s, ikw_acc[IDX_DIM:IKW], IDX_HEADS ** -0.5 * IDX_DIM ** -0.5).then_inc(iws_ready, 1)
            act.copy(ik_t[0:IDX_DIM], ikw_acc[0:IDX_DIM]).then_inc(evac[0], 1)
            split(5, 1, 1)
            act.wait_ge(small_done, 3)
            act.copy(ab_t[:], bank[1][:, 0:KW]).then_inc(small_ready, 1)
            act.copy(conv_t[:], bank[1][:, KW:KW + TAPS * KW].rearrange("p (r k) -> p r k", r=TAPS)).then_inc(small_ready, 1)
            for i in range(2):
                act.copy(ws_t[:, 4 * i:4 * i + 4], blk(bank[2 + i])).then_inc(small_ready, 1)
            act.wait_ge(table_done, 1)
            act.copy(table, bank[4][0:HEADS]).then_inc(table_ready, 1)
            act.wait_ge(iwt_done, 1)
            act.copy(iw[:], bank[5][:, 0:T * IDX_HEADS].rearrange("p (t h) -> p t h", t=T)).then_inc(iw_ready, 1)
            with act.Fori(0, 4) as c:
                for g in range(SUB):
                    if g == SUB - 1:
                        move(CH1 + c, chunk(keep, CZ + c, 0))
                    split_ahead(SUB1, c, SUB, g)
            act.wait_ge(bias_done, 1)
            for i in range(4):
                act.copy(keep[:, 0, (8 + i) * N:(9 + i) * N], bank[i]).then_inc(bias_ready, 1)
            with act.Fori(0, 8) as c:
                for g in range(SUB):
                    if g == 0:
                        act.copy(iq_s, block(keep, IQ, c)).then_inc(iq_ready, 1)
                    if g == 2:
                        act.wait_ge(iqt_done, c + 1)
                        act.copy(iq_t, bank[0][:, 0:SEQ]).then_inc(iqt_ready, 1)
                    if g == 4:
                        act.wait_ge(index_done, c + 1)
                        for h in range(2):
                            act.activation(relu[:, h], bank[1 + h][:, 0:384], ACT.Relu).then_inc(relu_ready, 1)
                    if g == SUB - 1:
                        move(CH2 + c, chunk(early, c, 0))
                    split_ahead(SUB2, c, SUB, g)
            for c in range(2):
                for g in range(SUB):
                    if c == 0 and g == 1:
                        act.activation(section(keep, CZ), section(keep, CZ), ACT.Silu).then_inc(silu_ready, 1)
                    if g == SUB - 1:
                        move(CH3 + c, chunk(keep, BC + c, 0))
                    split_ahead(SUB3, c, SUB, g)
            with act.Fori(0, 4) as c:
                for g in range(SUB):
                    if g == SUB - 1:
                        move(CH4 + c, chunk(early, BX + c, 0))
                    split_ahead(SUB4, c, SUB, g)
            act.wait_ge(evac[1], CH5)
            act.wait_ge(evac[0], CH5)
            act.activation(section(early, BZ), section(early, BZ), ACT.Silu).then_inc(silu_ready, 1)
            with act.Fori(0, 8) as c:
                for g in range(SUB):
                    if g == 0:
                        for w, slot in enumerate((Q, K)):
                            act.copy(qk_s[:, w], block(early, slot, c)).then_inc(qk_ready, 1)
                    if g == 2:
                        act.wait_ge(qkt_done, c + 1)
                        act.copy(qk_t, bank[0]).then_inc(qkt_ready, 1)
                    if g == 4:
                        act.wait_ge(soft_step, 4 * c + 4)
                        for i, part_ in enumerate((slice(0, P), slice(P, 384))):
                            act.activation(prob[:, part_], logit[:, part_], ACT.Exp, bias=nmax[:, i:i + 1],
                                           accum_out=rowsum[:, i:i + 1]).then_inc(prob_ready, 1)
                    if g == SUB - 1:
                        move(CH5 + c, chunk(keep, AZ + c, 0))
                    split_ahead(SUB5, c, SUB, g)
            act.wait_ge(evac[1], CH6)
            act.wait_ge(evac[0], CH6)
            act.activation(section(keep, AZ), section(keep, AZ), ACT.Silu).then_inc(silu_ready, 1)
            with act.Fori(0, 8) as c:
                for g in range(SUB):
                    if g == 0:
                        for w, slot in enumerate((BX, BG)):
                            act.copy(cg_s[:, w], block(early, slot, c)).then_inc(cg_ready, 1)
                    if g == 3:
                        act.copy(wsg, ws_t[:, bass.ds(c, 1)].rearrange("p a t -> p (a t)")).then_inc(wsg_ready, 1)
                    if g == SUB - 1:
                        move(CH6 + c, chunk(keep, GC + c, 0))
                    split_ahead(SUB6, c, SUB, g)
            for c in range(2):
                for g in range(SUB):
                    n = SUB * c + g
                    if n % 2:
                        i = n // 2
                        act.wait_ge(yt_done, i + 1)
                        act.copy(yh[:, 2 * i:2 * i + 2], bank[i % 2].rearrange("p (k t) -> p k t", k=2)).then_inc(yh_ready, 1)
                    if n % 4 == 2:
                        k = n // 2 - 1
                        if k == 0:
                            act.wait_ge(conv_step, 4 * KW)
                        act.copy(yh[:, 2 * KW + k:2 * KW + k + 2].rearrange("p k (t c) -> p k t c", t=T),
                                 keep[:, :, YB * N + k * P:YB * N + (k + 2) * P].rearrange("p t (k c) -> p k t c", c=P)
                                 ).then_inc(yh_ready, 1)
                    if g == SUB - 1:
                        move(CH7 + c, chunk(keep, GB + c, 0))
                    split_ahead(SUB7, c, SUB, g)
            act.wait_ge(evac[0], CHP)
            act.wait_ge(evac[1], CHP)
            def high_merged(j, i):
                act.wait_ge(mt_done, 2 * j + i + 1)
                act.copy(hh[:, bass.ds(4 * j + 2 * i, 2)], bank_m[i].rearrange("p (k t) -> p k t", k=2)).then_inc(mh_ready, 1)

            def outputs(j, first):
                for n in range(3 * SUBP):
                    if n % SUBP == 0:
                        gate = (GC, GA, GB)[n // SUBP]
                        here = keep[:, :, bass.ds((gate + j) * N, N)]
                        act.activation(here, here, ACT.Sigmoid).then_inc(sig_ready, 1)
                    if n in (2, 3) and not first:
                        high_merged(j - 1, n - 2)
                    split_ahead(SUBP0, j, 3 * SUBP, n)

            outputs(0, True)
            with act.Fori(1, 4) as j:
                outputs(j, False)

            def squares(j, t):
                act.wait_ge(xo_ready[t], j + 1)
                act.activation(part[:, t], x_o[:, t, bass.ds(j * N, N)], ACT.Square,
                               accum_out=ssq[:, t, bass.ds(j, 1)]).then_inc(ssq_ready, 1)

            for g in range(SUB):
                if g in (2, 3):
                    high_merged(3, g - 2)
                split_ahead(SUBO, 0, SUB, g)
            with act.Fori(1, 3) as j:
                for g in range(SUB):
                    if g == 1:
                        for t in range(T):
                            squares(j - 1, t)
                    split_ahead(SUBO, j, SUB, g)
            for g in range(SUB - RING):
                if g == 1:
                    for t in range(T):
                        squares(2, t)
                split_ahead(SUBO, 3, SUB, g)
            act.activation(inv_root, inv[:, 0:1], ACT.Sqrt)
            for t in range(T):
                squares(3, t)
                act.wait_ge(var_done, 2 * T + t + 1)
                act.activation(root[:, t:t + 1], var[:, t:t + 1], ACT.Sqrt).then_inc(root_done, 1)
            act.wait_ge(xf_ready, 4 * T)
            act.wait_ge(inv_ready, 2 * T)
            for i in (1, 3):
                here = y_out[:, 1, i * N:(i + 1) * N]
                act.activation(here, here, ACT.Copy, scale=inv[:, 1:2]).then_inc(y_ready[1], 1)

        @block_.vector
        def _(dve):
            def split(n, slot, width=KS * N):
                dve.wait_ge(high_split, n + 1)
                dve.tensor_tensor(wl[:, slot, 0:width], raw[:, slot, 0:width], wh[:, slot, 0:width].bitcast(F32),
                                  ALU.subtract).then_inc(low_split, 1)

            def split_ahead(base, it, per, g):
                split(base + per * it + g + RING, (SUB1 + g) % RING)

            def move(q, last, dst):
                dve.wait_ge(sub_used, last + 1)
                dve.tensor_copy(dst, acc[1]).then_inc(evac[1], 1)

            steps, invs = [0], [0]

            def rsqrt(t):
                v, r, i, s = (a[:, t:t + 1] for a in (var, root, inv, tmp2))
                for op in (lambda: dve.reciprocal(i, r),
                           lambda: dve.scalar_tensor_tensor(s, i, v, i, ALU.mult, ALU.mult),
                           lambda: dve.tensor_scalar(s, s, -0.5, 1.5, ALU.mult, ALU.add)):
                    op().then_inc(norm_step, 1)
                    steps[0] += 1
                    dve.wait_ge(norm_step, steps[0])
                invs[0] += 1
                dve.tensor_tensor(i, i, s, ALU.mult).then_inc(inv_ready, 1)
                dve.wait_ge(inv_ready, invs[0])

            dve.memset(one, 1.0).then_inc(const_ready, 1)

            def variance(t):
                dve.wait_ge(sq_done, 2 * t + 1)
                dve.tensor_scalar(tmp2[:, t:t + 1], ssq[:, t, 0:1], 1.0 / D, EPS, ALU.mult, ALU.add).then_inc(var_done, 1)
                dve.wait_ge(sq_done, 2 * t + 2)
                dve.wait_ge(var_done, 2 * t + 1)
                dve.scalar_tensor_tensor(var[:, t:t + 1], ssq[:, t, 1:2], 1.0 / D, tmp2[:, t:t + 1],
                                         ALU.mult, ALU.add).then_inc(var_done, 1)

            def normalise(t):
                dve.wait_ge(root_done, t + 1)
                dve.wait_ge(var_done, 2 * t + 2)
                rsqrt(t)
                for i in range(4):
                    c = slice(i * N, (i + 1) * N)
                    dve.tensor_scalar(xn[:, t, c], x_s[:, t, c], inv[:, t:t + 1], None, ALU.mult).then_inc(xn_ready, 1)

            variance(0)
            normalise(0)
            variance(1)
            normalise(1)
            dve.wait_ge(gt_ready, 1)
            for k in range(KD):
                if k in (0, KD // 2):
                    n = k // (KD // 2)
                    split(n, n, KW * IKW)
                dve.wait_ge(hh_ready, k + 1 + (k + 1) % 2)
                dve.scalar_tensor_tensor(hl[:, k], x_t[:, k], g_t[:, k:k + 1], hh[:, k].bitcast(F32),
                                         ALU.mult, ALU.subtract).then_inc(hl_ready, 1)
            for n in range(2, 4):
                split(n, n)
            split(4, 0)
            dve.wait_ge(evac[0], 1)
            dve.tensor_copy(ik_t[IDX_DIM:P], ik_t[0:IDX_DIM]).then_inc(evac[1], 1)
            split(5, 1)
            dve.memset(score, 0.0).then_inc(score_step, 1)
            with dve.Fori(0, 4) as c:
                for g in range(SUB):
                    if g == SUB - 1:
                        move(0, SUB1 + SUB * c + g, chunk(keep, CZ + c, 1))
                    split_ahead(SUB1, c, SUB, g)
            with dve.Fori(0, 8) as c:
                for g in range(SUB):
                    if g == 5:
                        for h in range(2):
                            dve.wait_ge(relu_ready, 2 * c + h + 1)
                            for t, s in enumerate((slice(0, P), slice(P, 384))):
                                if t == 0:
                                    dve.wait_ge(score_step, 4 * c + 2 * h + 1)
                                dve.scalar_tensor_tensor(score[:, s], relu[:, h, s], iw[:, t, bass.ds(2 * c + h, 1)],
                                                         score[:, s], ALU.mult, ALU.add).then_inc(score_step, 1)
                    if g == SUB - 1:
                        move(0, SUB2 + SUB * c + g, chunk(early, c, 1))
                    split_ahead(SUB2, c, SUB, g)
            for c in range(2):
                for g in range(SUB):
                    n = SUB * c + g
                    t, s = n % 2, (slice(0, P), slice(P, 384))[n % 2]
                    if n == 0:
                        dve.wait_ge(score_masked, 2)
                    if n >= 2:
                        dve.wait_ge(top_step, 2 * (n - 1))
                    dve.max(top8[:, t], score[:, s]).then_inc(top_step, 1)
                    dve.wait_ge(top_step, 2 * n + 1)
                    dve.match_replace(score[:, s], top8[:, t], score[:, s], TAKEN).then_inc(top_step, 1)
                    if g == SUB - 1:
                        move(0, SUB3 + n, chunk(keep, BC + c, 1))
                    split_ahead(SUB3, c, SUB, g)
            dve.wait_ge(top_step, 2 * 2 * TOPK // 8)
            dve.tensor_scalar(mask, score, 0.5 * TAKEN, NEG, ALU.is_gt, ALU.mult).then_inc(mask_ready, 1)
            with dve.Fori(0, 4) as c:
                for g in range(SUB):
                    if g == SUB - 1:
                        move(0, SUB4 + SUB * c + g, chunk(early, BX + c, 1))
                    split_ahead(SUB4, c, SUB, g)
            dve.wait_ge(evac[0], CH5)
            dve.wait_ge(evac[1], CH5)
            dve.tensor_tensor(section(early, BX), section(early, BX), section(keep, BC), ALU.mult).then_inc(gate_step, 1)
            dve.wait_ge(silu_ready, 2)
            dve.tensor_tensor(section(early, BG), section(early, BG), section(early, BZ), ALU.mult).then_inc(gate_step, 1)
            dve.wait_ge(bias_masked, 2 + 2 * HEADS)
            with dve.Fori(0, 8) as c:
                for g in range(SUB):
                    if g == 3:
                        dve.wait_ge(logit_done, c + 1)
                        dve.scalar_tensor_tensor(logit, bank[1][:, 0:384], SCALE,
                                                 bias_m[:, bass.ds(c, 1)].rearrange("p a s -> p (a s)"),
                                                 ALU.mult, ALU.add).then_inc(soft_step, 1)
                        dve.wait_ge(soft_step, 4 * c + 1)
                        dve.reduce_max(tmp2[:, 0:1], logit[:, 0:P], AX_X).then_inc(soft_step, 1)
                        dve.reduce_max(tmp2[:, 1:2], logit[:, P:], AX_X).then_inc(soft_step, 1)
                        dve.wait_ge(soft_step, 4 * c + 3)
                        dve.tensor_scalar(nmax, tmp2, -1.0, None, ALU.mult).then_inc(soft_step, 1)
                    if g == 5:
                        dve.wait_ge(probt_done, c + 1)
                        dve.tensor_copy(prob_t, bank[2][:, 0:384]).then_inc(probt_ready, 1)
                        dve.wait_ge(prob_ready, 2 * c + 2)
                        dve.reciprocal(rrow, rowsum).then_inc(yc_step, 1)
                    if g == 7:
                        dve.wait_ge(pv_done, c + 1)
                        dve.wait_ge(yc_step, 3 * c + 1)
                        for t in range(T):
                            here = keep[:, t, bass.ds(CZ * N + c * P, P)]
                            dve.scalar_tensor_tensor(here, bank[3][:, t * P:(t + 1) * P], rrow[:, t:t + 1], here,
                                                     ALU.mult, ALU.mult).then_inc(yc_step, 1)
                    if g == SUB - 1:
                        move(0, SUB5 + SUB * c + g, chunk(keep, AZ + c, 1))
                    split_ahead(SUB5, c, SUB, g)
            dve.wait_ge(silu_ready, 3)
            dve.tensor_tensor(section(keep, AU), section(keep, AU), section(keep, AZ), ALU.mult).then_inc(gate_step, 1)
            dve.wait_ge(gate_step, 3)
            with dve.Fori(0, 8) as c:
                for g in range(SUB):
                    if g == 2:
                        dve.wait_ge(cgt_done, c + 1)
                        tap = [conv_t[:, r, bass.ds(c, 1)] for r in range(TAPS)]
                        dve.tensor_scalar(conv_y, bank[0][:, 0:SEQ], tap[2], None, ALU.mult).then_inc(conv_step, 1)
                        for r in range(1, TAPS):
                            dve.wait_ge(conv_step, 4 * c + r)
                            dve.scalar_tensor_tensor(conv_y[:, r:], bank[0][:, 0:SEQ - r], tap[2 - r], conv_y[:, r:],
                                                     ALU.mult, ALU.add).then_inc(conv_step, 1)
                        dve.wait_ge(conv_step, 4 * c + 3)
                        dve.tensor_tensor(block(keep, YB, c), conv_y.rearrange("p (t s) -> p t s", t=T),
                                          bank[0][:, SEQ:].rearrange("p (t s) -> p t s", t=T), ALU.mult).then_inc(conv_step, 1)
                    if g == 5:
                        dve.wait_ge(mix_done, c + 1)
                        dve.scalar_tensor_tensor(block(keep, AU, c), bank[1][:, 0:SEQ].rearrange("p (t s) -> p t s", t=T),
                                                 ab_t[:, bass.ds(c, 1)], block(keep, AU, c), ALU.add,
                                                 ALU.mult).then_inc(ya_ready, 1)
                    if g == SUB - 1:
                        move(0, SUB6 + SUB * c + g, chunk(keep, GC + c, 1))
                    split_ahead(SUB6, c, SUB, g)
            dve.wait_ge(conv_step, 4 * KW)
            for c in range(2):
                for g in range(SUB):
                    n = SUB * c + g
                    done = (n + 1) // 2 + (n + 2) // 4
                    if n % 2:
                        i = n // 2
                        dve.wait_ge(yh_ready, done)
                        dve.tensor_tensor(yl[:, 2 * i:2 * i + 2], bank[i % 2].rearrange("p (k t) -> p k t", k=2),
                                          yh[:, 2 * i:2 * i + 2].bitcast(F32), ALU.subtract).then_inc(yl_ready, 1)
                    if n % 4 == 2:
                        k = n // 2 - 1
                        dve.wait_ge(yh_ready, done)
                        dve.tensor_tensor(yl[:, 2 * KW + k:2 * KW + k + 2].rearrange("p k (t c) -> p k t c", t=T),
                                          keep[:, :, YB * N + k * P:YB * N + (k + 2) * P].rearrange("p t (k c) -> p k t c", c=P),
                                          yh[:, 2 * KW + k:2 * KW + k + 2].bitcast(F32).rearrange("p k (t c) -> p k t c", t=T),
                                          ALU.subtract).then_inc(yl_ready, 1)
                    if g == SUB - 1:
                        move(0, SUB7 + n, chunk(keep, GB + c, 1))
                    split_ahead(SUB7, c, SUB, g)
            def low_merged(j, i):
                dve.wait_ge(mh_ready, 2 * j + i + 1)
                here = bass.ds(4 * j + 2 * i, 2)
                dve.tensor_tensor(hl[:, here], bank_m[i].rearrange("p (k t) -> p k t", k=2), hh[:, here].bitcast(F32),
                                  ALU.subtract).then_inc(ml_ready, 1)

            def outputs(j, first):
                for n in range(3 * SUBP):
                    if n in (2, 3) and not first:
                        low_merged(j - 1, n - 2)
                    if n % SUBP == SUBP - 1:
                        b = n // SUBP
                        gate = (GC, GA, GB)[b]
                        dst = merged if b == 0 else part
                        dve.wait_ge(sig_ready, 3 * j + b + 1)
                        dve.wait_ge(tile0_done, CHP + 3 * j + b)
                        dve.tensor_tensor(dst[:, 0], acc_p[b][0], keep[:, 0, bass.ds((gate + j) * N, N)], ALU.mult).then_inc(evac[0], 1)
                        dve.wait_ge(sub_used, SUBP0 + 3 * SUBP * j + n + 1)
                        dve.tensor_tensor(dst[:, 1], acc_p[b][1], keep[:, 1, bass.ds((gate + j) * N, N)], ALU.mult).then_inc(evac[1], 1)
                        for t in range(T if b else 0):
                            dve.wait_ge(evac[t], CHP + 3 * j + b + 1)
                            if b == 2:
                                dve.wait_ge(merge_step, T * j + t + 1)
                            dve.tensor_tensor(merged[:, t], merged[:, t], part[:, t],
                                              ALU.add).then_inc(merge_step if b == 1 else merge_ready, 1)
                    split_ahead(SUBP0, j, 3 * SUBP, n)

            outputs(0, True)
            with dve.Fori(1, 4) as j:
                outputs(j, False)

            def residual(j, t):
                here = x_o[:, t, bass.ds(j * N, N)]
                dve.tensor_tensor(here, psum[:, bass.ds(T * j + t, 1)].rearrange("p a n -> p (a n)"), here,
                                  ALU.add).then_inc(xo_ready[t], 1)

            dve.wait_ge(xo_loaded, 16)
            for g in range(SUB):
                if g in (2, 3):
                    low_merged(3, g - 2)
                split_ahead(SUBO, 0, SUB, g)
            with dve.Fori(1, 3) as j:
                for g in range(SUB):
                    if g == 0:
                        dve.wait_ge(sub_used, SUBO + SUB * j)
                        for t in range(T):
                            residual(j - 1, t)
                    split_ahead(SUBO, j, SUB, g)
            for g in range(SUB - RING):
                if g == 0:
                    dve.wait_ge(sub_used, SUBO + SUB * 3)
                    for t in range(T):
                        residual(2, t)
                split_ahead(SUBO, 3, SUB, g)
            dve.wait_ge(ssq_ready, T * 3)
            dve.reduce_sum(tmp2, ssq[:, :, 0:3], AX_X).then_inc(norm_step, 1)
            steps[0] += 1
            dve.wait_ge(norm_step, steps[0])
            dve.tensor_scalar(partial, tmp2, 1.0 / D, EPS, ALU.mult, ALU.add).then_inc(norm_step, 1)
            steps[0] += 1
            for t in range(T):
                if t == 0:
                    dve.wait_ge(tile0_done, CHO + 3)
                else:
                    dve.wait_ge(sub_used, SUBO + SUB * 4)
                residual(3, t)
                dve.wait_ge(norm_step, steps[0])
                dve.wait_ge(ssq_ready, T * 3 + t + 1)
                dve.scalar_tensor_tensor(var[:, t:t + 1], ssq[:, t, 3:4], 1.0 / D, partial[:, t:t + 1],
                                         ALU.mult, ALU.add).then_inc(var_done, 1)
                dve.wait_ge(root_done, T + t + 1)
                dve.wait_ge(var_done, 2 * T + t + 1)
                rsqrt(t)
                for i in (range(4) if t == 0 else (0, 2)):
                    dve.wait_ge(xf_ready, 3 * T + t + 1)
                    here = y_out[:, t, i * N:(i + 1) * N]
                    dve.tensor_scalar(here, here, inv[:, t:t + 1], None, ALU.mult).then_inc(y_ready[0], 1)

        @block_.tensor
        def _(pe):
            def product(n, slot, g, last, high, low, k0, q, ks=KS, free=None, dst=acc, tiles=range(T)):
                pe.wait_ge(low_split, n + 1)
                w_h, w_l = (w[:, slot].rearrange("p (k c) -> p k c", k=ks) for w in (wh, wl))
                for t in tiles:
                    tok = slice(t * P, (t + 1) * P)
                    if g == 0 and free is not None:
                        pe.wait_ge(free[t], q)
                    for j in range(ks):
                        h, l = high[:, k0 + j, tok], low[:, k0 + j, tok]
                        start, stop = g == 0 and j == 0, last and j == ks - 1
                        pe.matmul(dst[t], h, w_h[:, j], start=start, stop=False)
                        pe.matmul(dst[t], h, w_l[:, j], start=False, stop=False)
                        mm = pe.matmul(dst[t], l, w_h[:, j], start=False, stop=stop)
                    if last and t == 0:
                        mm.then_inc(tile0_done, 1)
                if T - 1 in tiles:
                    mm.then_inc(sub_used, 1)

            def transpose(dst, src):
                return pe.transpose(dst, src, ident[:])

            pe.wait_ge(ident_loaded, 16)
            pe.wait_ge(g_loaded, 16)
            pe.transpose(bank[5][:, 0:KD], g_s, ident[0:KD, 0:KD]).then_inc(gt_done, 1)
            for i in range(WARM_UP):
                transpose(bank[4][:, 0:P], ident[:])
            pe.wait_ge(gt_ready, 1)
            for t in range(T):
                for k in range(KD):
                    if k % 4 == 0:
                        pe.wait_ge(xn_ready, 4 * t + k // 4 + 1)
                    mm = transpose(x_t[:, k, t * P:(t + 1) * P], xn[:, t, k * P:(k + 1) * P])
                    if t == 1 and k % 2:
                        mm.then_inc(xt_done, 1)
            for k in range(KD):
                n, i = k // KW, k % KW
                if i == 0:
                    pe.wait_ge(low_split, n + 1)
                pe.wait_ge(hl_ready, max(k + 1, 2))
                w_h, w_l = (w[:, n, i * IKW:(i + 1) * IKW] for w in (wh, wl))
                pe.matmul(ikw_acc, w_h, hh[:, k], start=k == 0, stop=False)
                pe.matmul(ikw_acc, w_l, hh[:, k], start=False, stop=False)
                mm = pe.matmul(ikw_acc, w_h, hl[:, k], start=False, stop=k == KD - 1)
                if k == KW - 1:
                    mm.then_inc(sub_used, 1)
            mm.then_inc(sub_used, 1)
            some = KW + TAPS * KW
            pe.wait_ge(small_loaded, 16 * 6)
            pe.transpose(bank[1][:, 0:some], small[0:some], ident[0:some, 0:some]).then_inc(small_done, 1)
            for i in range(2):
                for j in range(4):
                    mm = transpose(bank[2 + i][:, j * P:(j + 1) * P], ws_s[:, (4 * i + j) * P:(4 * i + j + 1) * P])
                mm.then_inc(small_done, 1)
            pe.matmul(bank[4][0:HEADS], rel, onehot, start=True, stop=True).then_inc(table_done, 1)
            pe.wait_ge(iws_ready, 1)
            for t in range(T):
                mm = pe.transpose(bank[5][:, t * IDX_HEADS:(t + 1) * IDX_HEADS], iw_s[:, t * P:(t + 1) * P],
                                  ident[IDX_DIM:IKW, IDX_DIM:IKW])
            mm.then_inc(iwt_done, 1)
            with pe.Fori(0, 4) as c:
                for g in range(SUB):
                    product(SUB1 + SUB * c + g, (SUB1 + g) % RING, g, g == SUB - 1, hh, hl, KS * g, CH1 + c, free=evac)
            pe.wait_ge(bias_loaded, 16)
            pe.wait_ge(iw_ready, 1)
            for i in range(4):
                mm = pe.matmul(bank[i], flip_s, bias_rev[:, i * N:(i + 1) * N], start=True, stop=True)
            mm.then_inc(bias_done, 1)
            with pe.Fori(0, 8) as c:
                for g in range(SUB):
                    product(SUB2 + SUB * c + g, (SUB1 + g) % RING, g, g == SUB - 1, hh, hl, KS * g, CH2 + c, free=evac)
                    if g == 1:
                        pe.wait_ge(bias_ready, 4)
                        pe.wait_ge(iq_ready, c + 1)
                        for t in range(T):
                            mm = transpose(bank[0][:, t * P:(t + 1) * P], iq_s[:, t])
                        mm.then_inc(iqt_done, 1)
                    if g == 3:
                        pe.wait_ge(iqt_ready, c + 1)
                        for h in range(2):
                            half = slice(h * IDX_DIM, (h + 1) * IDX_DIM)
                            pe.matmul(bank[1 + h][:, 0:P], iq_t[half, 0:P], ik_t[half, 0:P], start=True, stop=True)
                            mm = pe.matmul(bank[1 + h][:, P:384], iq_t[half, P:SEQ], ik_t[half], start=True, stop=True)
                        mm.then_inc(index_done, 1)
            for c in range(2):
                for g in range(SUB):
                    product(SUB3 + SUB * c + g, (SUB1 + g) % RING, g, g == SUB - 1, hh, hl, KS * g, CH3 + c, free=evac)
            with pe.Fori(0, 4) as c:
                for g in range(SUB):
                    product(SUB4 + SUB * c + g, (SUB1 + g) % RING, g, g == SUB - 1, hh, hl, KS * g, CH4 + c, free=evac)
            with pe.Fori(0, 8) as c:
                for g in range(SUB):
                    product(SUB5 + SUB * c + g, (SUB1 + g) % RING, g, g == SUB - 1, hh, hl, KS * g, CH5 + c, free=evac)
                    if g == 1:
                        pe.wait_ge(qk_ready, 2 * c + 2)
                        for w in range(2):
                            for t in range(T):
                                mm = transpose(bank[0][:, (2 * w + t) * P:(2 * w + t + 1) * P], qk_s[:, w, t])
                        mm.then_inc(qkt_done, 1)
                    if g == 2:
                        pe.wait_ge(qkt_ready, c + 1)
                        pe.matmul(bank[1][:, 0:P], qk_t[:, 0:P], qk_t[:, SEQ:SEQ + P], start=True, stop=True)
                        pe.matmul(bank[1][:, P:384], qk_t[:, P:SEQ], qk_t[:, SEQ:], start=True,
                                  stop=True).then_inc(logit_done, 1)
                    if g == 4:
                        pe.wait_ge(prob_ready, 2 * c + 2)
                        for i in range(3):
                            mm = transpose(bank[2][:, i * P:(i + 1) * P], prob[:, i * P:(i + 1) * P])
                        mm.then_inc(probt_done, 1)
                    if g == 6:
                        pe.wait_ge(probt_ready, c + 1)
                        v = [early[:, t, bass.ds(V * N + c * P, P)] for t in range(T)]
                        pe.matmul(bank[3][:, 0:P], prob_t[:, 0:P], v[0], start=True, stop=True)
                        pe.matmul(bank[3][:, P:SEQ], prob_t[:, P:SEQ], v[0], start=True, stop=False)
                        pe.matmul(bank[3][:, P:SEQ], prob_t[:, SEQ:384], v[1], start=False,
                                  stop=True).then_inc(pv_done, 1)
            with pe.Fori(0, 8) as c:
                for g in range(SUB):
                    product(SUB6 + SUB * c + g, (SUB1 + g) % RING, g, g == SUB - 1, hh, hl, KS * g, CH6 + c, free=evac)
                    if g == 1:
                        pe.wait_ge(cg_ready, 2 * c + 2)
                        for w in range(2):
                            for t in range(T):
                                mm = transpose(bank[0][:, (2 * w + t) * P:(2 * w + t + 1) * P], cg_s[:, w, t])
                        mm.then_inc(cgt_done, 1)
                    if g == 3:
                        pe.wait_ge(wsg_ready, c + 1)
                        pe.matmul(bank[1][:, 0:SEQ], wsg, block(keep, AV, c), start=True, stop=True).then_inc(mix_done, 1)
            pe.wait_ge(ya_ready, KW)
            for c in range(2):
                for g in range(SUB):
                    n = SUB * c + g
                    product(SUB7 + n, (SUB1 + g) % RING, g, g == SUB - 1, hh, hl, KS * g, CH7 + c, free=evac)
                    if n % 2 == 0:
                        i = n // 2
                        slot, k = (CZ, AU)[i // 4], 2 * (i % 4)
                        if i >= 2:
                            pe.wait_ge(yl_ready, yl_after(i - 2))
                        for j in range(2):
                            for t in range(T):
                                mm = transpose(bank[i % 2][:, (2 * j + t) * P:(2 * j + t + 1) * P],
                                               keep[:, t, slot * N + (k + j) * P:slot * N + (k + j + 1) * P])
                        mm.then_inc(yt_done, 1)
            def transpose_merged(j):
                pe.wait_ge(merge_ready, T * j + T)
                for i in range(2):
                    for k in range(2):
                        for t in range(T):
                            mm = transpose(bank_m[i][:, (2 * k + t) * P:(2 * k + t + 1) * P],
                                           merged[:, t, (2 * i + k) * P:(2 * i + k + 1) * P])
                    mm.then_inc(mt_done, 1)

            def outputs(j, first):
                for n in range(3 * SUBP):
                    b, g = n // SUBP, n % SUBP
                    free = evac if b == 0 or not first else None
                    product(SUBP0 + 3 * SUBP * j + n, (SUB1 + n) % RING, g, g == SUBP - 1, yh, yl,
                            b * KW + KS * g, CHP + 3 * j + b - (0 if first else 2), free=free, dst=acc_p[b])
                    if n == 1 and not first:
                        transpose_merged(j - 1)

            pe.wait_ge(yl_ready, 12)
            outputs(0, True)
            with pe.Fori(1, 4) as j:
                outputs(j, False)

            def acc_o(j):
                return [psum[:, bass.ds(T * j + t, 1)].rearrange("p a n -> p (a n)") for t in range(T)]

            pe.wait_ge(ml_ready, 6)
            for g in range(SUB):
                if g == SUB - 2:
                    pe.wait_ge(ml_ready, 8)
                product(SUBO + g, (SUB1 + g) % RING, g, g == SUB - 1, hh, hl, KS * g, CHO - 2, free=evac, dst=acc_o(0))
                if g == 1:
                    transpose_merged(3)
            with pe.Fori(1, 3) as j:
                for g in range(SUB):
                    product(SUBO + SUB * j + g, (SUB1 + g) % RING, g, g == SUB - 1, hh, hl, KS * g, 0, dst=acc_o(j))
            for tiles, gs in ((range(T), range(RING)), ((0,), range(RING, SUB)), ((1,), range(RING, SUB))):
                for g in gs:
                    product(SUBO + SUB * 3 + g, (SUB1 + g) % RING, g, g == SUB - 1, hh, hl, KS * g, 0, dst=acc_o(3),
                            tiles=tiles)


def yl_after(i):
    n = 2 * i + 1
    return (n + 1) // 2 + (n + 2) // 4


_INS = ['x', 'norm_g', 'w_in', 'a_ws', 'a_b', 'b_conv', 'p_a', 'p_b', 'p_c', 'w_o', 'rel_bias', 'final_g']


def _constants():
    import numpy as np
    eye = np.eye(P, dtype=np.float32)
    dist = np.maximum(SEQ - 1 - np.arange(N), 0)
    exact = BUCKETS // 2
    large = exact + (np.log(np.maximum(dist, 1) / exact) / np.log(MAX_DISTANCE / exact) * (BUCKETS - exact)).astype(np.int64)
    bucket = np.where(dist < exact, dist, np.minimum(large, BUCKETS - 1))
    onehot = (np.arange(BUCKETS)[:, None] == bucket[None]).astype(np.float32)
    return {"identity": eye, "flip": np.ascontiguousarray(eye[::-1]), "buckets": onehot}


def kernel(**inputs):
    import numpy as np
    import concourse.bacc as bacc
    from concourse.bass_utils import run_bass_kernel_spmd

    nc = bacc.Bacc("TRN2", target_bir_lowering=False, num_devices=1)
    arrays = {name: np.ascontiguousarray(inputs[name]) for name in _INS}
    arrays.update(_constants())
    args = [nc.dram_tensor(name, a.shape, F32, kind="ExternalInput").ap() for name, a in arrays.items()]
    out = nc.dram_tensor("out", (1, SEQ, D), F32, kind="ExternalOutput").ap()
    trunk(nc, *args, out)
    r = run_bass_kernel_spmd(nc, [arrays], core_ids=[0])
    return r.results[0]["out"]
```
